# Optimizing a Trainium2 kernel written in Bass

```python
import math
import jax, jax.numpy as jnp
from jax import lax
import numpy as np

D_MODEL = 1024
BATCH = 1
SEQ = 256
DEPTH = 2

CTX_LEN = 256
GRID_W = 64
HEAD_DIM = 64
FOURIER_GROUPS = 6
FOURIER_WIDTH = FOURIER_GROUPS * HEAD_DIM
SWA_Q_HEADS = 8
SWA_KV_HEADS = 2
SWA_WIDTH = SWA_Q_HEADS * HEAD_DIM
WINDOW = 128
BLOCK = 128
CONV_WIDTH = 384
CONV_K = 3
DIFF_HEADS = 4
DIFF_V_DIM = 2 * HEAD_DIM
DIFF_WIDTH = DIFF_HEADS * DIFF_V_DIM
N_BRANCHES = 4
ROPE_BASE = 10000.0
NORM_EPS = 1e-6
NEG_INF = -1e30

IN_NAMES = ("a_x", "b_q", "b_k", "b_v", "c_x", "c_b", "c_c", "d_q", "d_k", "d_v",
            "z_a", "z_b", "z_c", "z_d", "m_g")
IN_SPLITS = (
    FOURIER_WIDTH,
    SWA_WIDTH, SWA_KV_HEADS * HEAD_DIM, SWA_KV_HEADS * HEAD_DIM,
    CONV_WIDTH, CONV_WIDTH, CONV_WIDTH,
    DIFF_HEADS * 2 * HEAD_DIM, DIFF_HEADS * 2 * HEAD_DIM, DIFF_WIDTH,
    FOURIER_WIDTH, SWA_WIDTH, CONV_WIDTH, DIFF_WIDTH,
    N_BRANCHES * D_MODEL,
)
IN_WIDTH = sum(IN_SPLITS)

kernel_name = "hybrid_fourier_swa_conv_diffattn_dit"

def rms_norm(t, gain):
    tf = t.astype(jnp.float32)
    y = tf * lax.rsqrt(jnp.mean(tf * tf, axis=-1, keepdims=True) + NORM_EPS)
    return (y * gain.astype(jnp.float32)).astype(t.dtype)

def rope_tables(n):
    rows = n // GRID_W
    row = jnp.broadcast_to(jnp.arange(rows, dtype=jnp.float32)[:, None], (rows, GRID_W)).reshape(-1)
    col = jnp.broadcast_to(jnp.arange(GRID_W, dtype=jnp.float32)[None, :], (rows, GRID_W)).reshape(-1)
    nf = HEAD_DIM // 4
    inv = ROPE_BASE ** (-jnp.arange(nf, dtype=jnp.float32) / nf)
    ar = row[:, None] * inv[None, :]
    ac = col[:, None] * inv[None, :]
    cos = jnp.concatenate([jnp.cos(ar), jnp.cos(ar), jnp.cos(ac), jnp.cos(ac)], axis=-1)
    sin = jnp.concatenate([jnp.sin(ar), jnp.sin(ar), jnp.sin(ac), jnp.sin(ac)], axis=-1)
    return cos, sin

def apply_rope(t, cos, sin):
    shape = (1, t.shape[1]) + (1,) * (t.ndim - 3) + (HEAD_DIM,)
    cs = cos.reshape(shape).astype(t.dtype)
    sn = sin.reshape(shape).astype(t.dtype)
    t1, t2, t3, t4 = jnp.split(t, 4, axis=-1)
    rot = jnp.concatenate([-t2, t1, -t4, t3], axis=-1)
    return t * cs + rot * sn

def in_project(h, w):
    idx = np.cumsum(np.array(IN_SPLITS))[:-1].tolist()
    parts = jnp.split(h @ w, idx, axis=-1)
    return dict(zip(IN_NAMES, parts))

def fourier_mix(u):
    b, n, _ = u.shape
    ug = u.astype(jnp.float32).reshape(b, n, FOURIER_GROUPS, HEAD_DIM)
    f = jnp.fft.fft2(ug, axes=(1, 3), norm="ortho").real
    return f.reshape(b, n, FOURIER_WIDTH).astype(u.dtype)

def short_conv(u_x, u_b, u_c, w):
    u = u_c * u_x
    n = u.shape[1]
    half = CONV_K // 2
    up = jnp.pad(u, ((0, 0), (half, half), (0, 0)))
    conv = sum(up[:, j:j + n] * w[j] for j in range(CONV_K))
    return u_b * conv

def window_attn_latent(q, k, v, kc, vc, sink):
    b, n, hq, d = q.shape
    hkv = k.shape[2]
    g = hq // hkv
    nb = n // BLOCK
    qb = q.reshape(b, nb, BLOCK, hkv, g, d)

    def band(t):
        tp = jnp.pad(t, ((0, 0), (BLOCK, BLOCK), (0, 0), (0, 0))).reshape(b, nb + 2, BLOCK, hkv, d)
        return jnp.concatenate([tp[:, :-2], tp[:, 1:-1], tp[:, 2:]], axis=2)

    kw, vw = band(k), band(v)
    qi = jnp.arange(BLOCK)[:, None]
    kj = jnp.arange(3 * BLOCK)[None, :]
    in_band = jnp.abs(kj - BLOCK - qi) <= WINDOW
    kpos = jnp.arange(nb)[:, None] * BLOCK + jnp.arange(3 * BLOCK)[None, :] - BLOCK
    valid = (kpos >= 0) & (kpos < n)
    mask = in_band[None] & valid[:, None, :]
    scale = HEAD_DIM ** -0.5
    s_loc = jnp.einsum("bnqhgd,bnkhd->bnhgqk", qb, kw).astype(jnp.float32) * scale
    s_loc = jnp.where(mask[None, :, None, None], s_loc, NEG_INF)
    s_ctx = jnp.einsum("bnqhgd,blhd->bnhgql", qb, kc).astype(jnp.float32) * scale
    sk = sink.astype(jnp.float32).reshape(1, 1, hkv, g, 1, 1)
    m = jnp.maximum(jnp.maximum(s_loc.max(-1, keepdims=True), s_ctx.max(-1, keepdims=True)), sk)
    p_loc = jnp.exp(s_loc - m)
    p_ctx = jnp.exp(s_ctx - m)
    inv = 1.0 / (p_loc.sum(-1, keepdims=True) + p_ctx.sum(-1, keepdims=True) + jnp.exp(sk - m))
    o = (jnp.einsum("bnhgqk,bnkhd->bnqhgd", (p_loc * inv).astype(v.dtype), vw)
         + jnp.einsum("bnhgql,blhd->bnqhgd", (p_ctx * inv).astype(v.dtype), vc))
    return o.reshape(b, n, hq * d)

def ctx_sink_attn(q, k, v, sink):
    b, l, hq, d = q.shape
    hkv = k.shape[2]
    g = hq // hkv
    qg = q.reshape(b, l, hkv, g, d)
    s = jnp.einsum("bqhgd,bkhd->bhgqk", qg, k).astype(jnp.float32) * (HEAD_DIM ** -0.5)
    sk = sink.astype(jnp.float32).reshape(1, hkv, g, 1, 1)
    m = jnp.maximum(s.max(-1, keepdims=True), sk)
    p = jnp.exp(s - m)
    p = p / (p.sum(-1, keepdims=True) + jnp.exp(sk - m))
    o = jnp.einsum("bhgqk,bkhd->bqhgd", p.astype(v.dtype), v)
    return o.reshape(b, l, hq * d)

def diff_attn_block(q, k, v, lam):
    s = jnp.einsum("bqhcd,bkhcd->bhcqk", q, k).astype(jnp.float32) * (HEAD_DIM ** -0.5)
    p = jax.nn.softmax(s, axis=-1)
    a = p[:, :, 0] - lam * p[:, :, 1]
    return jnp.einsum("bhqk,bkhe->bqhe", a.astype(v.dtype), v)

def diff_attn_latent(q, k, v, kc, vc, lam):
    b, n, h, _, d = q.shape
    nb = n // BLOCK
    k_all = jnp.concatenate([kc, k], axis=1)
    v_all = jnp.concatenate([vc, v], axis=1)
    qb = jnp.moveaxis(q.reshape(b, nb, BLOCK, h, 2, d), 1, 0)
    o = lax.map(lambda qq: diff_attn_block(qq, k_all, v_all, lam), qb)
    return jnp.moveaxis(o, 0, 1).reshape(b, n, h, DIFF_V_DIM)

def diff_out(o, subln_g, lam_init):
    b, n, h, e = o.shape
    return (rms_norm(o, subln_g) * (1.0 - lam_init)).reshape(b, n, h * e)

def merge(ys, zs, m_g, w_os, w_out_l):
    gates = jnp.split(jax.nn.sigmoid(m_g.astype(jnp.float32)).astype(m_g.dtype), N_BRANCHES, axis=-1)
    mixed = sum(gt * ((y * jax.nn.silu(z)) @ w) for gt, y, z, w in zip(gates, ys, zs, w_os))
    return mixed @ w_out_l

def setup_inputs(seed: int = 0) -> dict:
    key = jax.random.key(seed)
    ks = jax.random.split(key, 24)
    d = D_MODEL

    def nrm(k, shape, s):
        return jax.random.normal(k, shape, jnp.float32) * s

    return {
        "x": nrm(ks[0], (BATCH, SEQ, d), 1.0),
        "c": nrm(ks[1], (BATCH, d), 1.0),
        "ctx": nrm(ks[2], (BATCH, CTX_LEN, d), 1.0),
        "c_ctx": nrm(ks[3], (d,), 1.0),
        "norm_g": 1.0 + nrm(ks[4], (DEPTH, d), 0.02),
        "w_mod": nrm(ks[5], (DEPTH, d, 3 * d), 0.5 * d ** -0.5),
        "b_mod": nrm(ks[6], (DEPTH, 3 * d), 0.02),
        "w_in": nrm(ks[7], (DEPTH, d, IN_WIDTH), d ** -0.5),
        "q_norm_b": 1.0 + nrm(ks[8], (DEPTH, HEAD_DIM), 0.02),
        "k_norm_b": 1.0 + nrm(ks[9], (DEPTH, HEAD_DIM), 0.02),
        "sink_b": nrm(ks[10], (DEPTH, SWA_Q_HEADS), 0.5),
        "conv_w": nrm(ks[11], (DEPTH, CONV_K, CONV_WIDTH), CONV_K ** -0.5),
        "q_norm_d": 1.0 + nrm(ks[12], (DEPTH, HEAD_DIM), 0.02),
        "k_norm_d": 1.0 + nrm(ks[13], (DEPTH, HEAD_DIM), 0.02),
        "lam_q1": nrm(ks[14], (DEPTH, HEAD_DIM), 0.1),
        "lam_k1": nrm(ks[15], (DEPTH, HEAD_DIM), 0.1),
        "lam_q2": nrm(ks[16], (DEPTH, HEAD_DIM), 0.1),
        "lam_k2": nrm(ks[17], (DEPTH, HEAD_DIM), 0.1),
        "subln_d": 1.0 + nrm(ks[18], (DEPTH, DIFF_V_DIM), 0.02),
        "w_o_a": nrm(ks[19], (DEPTH, FOURIER_WIDTH, d), FOURIER_WIDTH ** -0.5),
        "w_o_b": nrm(ks[20], (DEPTH, SWA_WIDTH, d), SWA_WIDTH ** -0.5),
        "w_o_c": nrm(ks[21], (DEPTH, CONV_WIDTH, d), CONV_WIDTH ** -0.5),
        "w_o_d": nrm(ks[22], (DEPTH, DIFF_WIDTH, d), DIFF_WIDTH ** -0.5),
        "w_out": nrm(ks[23], (DEPTH, d, d), d ** -0.5),
    }

def reference(x, c, ctx, c_ctx, norm_g, w_mod, b_mod, w_in, q_norm_b, k_norm_b, sink_b, conv_w,
              q_norm_d, k_norm_d, lam_q1, lam_k1, lam_q2, lam_k2, subln_d,
              w_o_a, w_o_b, w_o_c, w_o_d, w_out):
    b, n, _ = x.shape
    lc = ctx.shape[1]
    cos, sin = rope_tables(n)
    for l in range(DEPTH):
        last = l == DEPTH - 1
        shift, scale, gate = jnp.split(jax.nn.silu(c) @ w_mod[l] + b_mod[l], 3, axis=-1)
        shift_c, scale_c, gate_c = jnp.split(jax.nn.silu(c_ctx) @ w_mod[l] + b_mod[l], 3, axis=-1)
        h = rms_norm(x, norm_g[l]) * (1.0 + scale[:, None]) + shift[:, None]
        hc = rms_norm(ctx, norm_g[l]) * (1.0 + scale_c) + shift_c
        p = in_project(h, w_in[l])
        pc = in_project(hc, w_in[l])

        lam_init = 0.8 - 0.6 * math.exp(-0.3 * l)
        lam = (jnp.exp(jnp.sum(lam_q1[l].astype(jnp.float32) * lam_k1[l].astype(jnp.float32)))
               - jnp.exp(jnp.sum(lam_q2[l].astype(jnp.float32) * lam_k2[l].astype(jnp.float32)))
               + lam_init)

        kc_b = rms_norm(pc["b_k"].reshape(b, lc, SWA_KV_HEADS, HEAD_DIM), k_norm_b[l])
        vc_b = pc["b_v"].reshape(b, lc, SWA_KV_HEADS, HEAD_DIM)
        kc_d = rms_norm(pc["d_k"].reshape(b, lc, DIFF_HEADS, 2, HEAD_DIM), k_norm_d[l])
        vc_d = pc["d_v"].reshape(b, lc, DIFF_HEADS, DIFF_V_DIM)

        y_a = fourier_mix(p["a_x"])
        q_b = apply_rope(rms_norm(p["b_q"].reshape(b, n, SWA_Q_HEADS, HEAD_DIM), q_norm_b[l]), cos, sin)
        k_b = apply_rope(rms_norm(p["b_k"].reshape(b, n, SWA_KV_HEADS, HEAD_DIM), k_norm_b[l]), cos, sin)
        v_b = p["b_v"].reshape(b, n, SWA_KV_HEADS, HEAD_DIM)
        y_b = window_attn_latent(q_b, k_b, v_b, kc_b, vc_b, sink_b[l])
        y_c = short_conv(p["c_x"], p["c_b"], p["c_c"], conv_w[l])
        q_d = apply_rope(rms_norm(p["d_q"].reshape(b, n, DIFF_HEADS, 2, HEAD_DIM), q_norm_d[l]), cos, sin)
        k_d = apply_rope(rms_norm(p["d_k"].reshape(b, n, DIFF_HEADS, 2, HEAD_DIM), k_norm_d[l]), cos, sin)
        v_d = p["d_v"].reshape(b, n, DIFF_HEADS, DIFF_V_DIM)
        y_d = diff_out(diff_attn_latent(q_d, k_d, v_d, kc_d, vc_d, lam), subln_d[l], lam_init)
        out = merge([y_a, y_b, y_c, y_d], [p["z_a"], p["z_b"], p["z_c"], p["z_d"]], p["m_g"],
                    [w_o_a[l], w_o_b[l], w_o_c[l], w_o_d[l]], w_out[l])
        x_next = x + gate[:, None] * out

        if not last:
            yc_a = fourier_mix(pc["a_x"])
            qc_b = rms_norm(pc["b_q"].reshape(b, lc, SWA_Q_HEADS, HEAD_DIM), q_norm_b[l])
            yc_b = ctx_sink_attn(qc_b, kc_b, vc_b, sink_b[l])
            yc_c = short_conv(pc["c_x"], pc["c_b"], pc["c_c"], conv_w[l])
            qc_d = rms_norm(pc["d_q"].reshape(b, lc, DIFF_HEADS, 2, HEAD_DIM), q_norm_d[l])
            yc_d = diff_out(diff_attn_block(qc_d, kc_d, vc_d, lam), subln_d[l], lam_init)
            out_c = merge([yc_a, yc_b, yc_c, yc_d], [pc["z_a"], pc["z_b"], pc["z_c"], pc["z_d"]], pc["m_g"],
                          [w_o_a[l], w_o_b[l], w_o_c[l], w_o_d[l]], w_out[l])
            ctx = ctx + gate_c * out_c
        x = x_next
    return x


_drawn_inputs = setup_inputs


def setup_inputs(seed=0):
    import zlib

    import numpy as np

    out = dict(_drawn_inputs(seed))
    spreads = {}
    factors = {'norm_g': 6.379,
     'q_norm_b': 64.0,
     'k_norm_b': 64.0,
     'sink_b': 8.0,
     'q_norm_d': 64.0,
     'k_norm_d': 58.53,
     'lam_q1': 13.995,
     'lam_k1': 31.162,
     'lam_q2': 4.548,
     'lam_k2': 6.142,
     'subln_d': 64.0}
    for name, (base, spread) in spreads.items():
        noise = np.random.default_rng([zlib.crc32(name.encode()), seed]).standard_normal(out[name].shape)
        drawn = base * np.exp(spread * noise) if base else spread * noise
        out[name] = __import__('jax').numpy.asarray(drawn.astype(out[name].dtype))
    for name, factor in factors.items():
        out[name] = (out[name] * factor).astype(out[name].dtype)
    return out
```

```python
import math
from contextlib import ExitStack

import numpy as np

import concourse.bass as bass
from concourse import mybir

F32 = mybir.dt.float32
F32R = mybir.dt.float32r
ALU = mybir.AluOpType
ACT = mybir.ActivationFunctionType
AX = mybir.AxisListType

P = 128
D = 1024
KD = D // P
SEQ = 256
CTX = 256
TOK = SEQ + CTX
DEPTH = 2
GRID_W = 64
HD = 64
FW, SW, KV, CW, DW = 384, 512, 128, 384, 512
WINDOW = 128
EPS = 1e-6
SCALE = HD ** -0.5
MASKED = -1e30
BIG = 2.0 ** 64

_NAMES = ("a_x", "b_q", "b_k", "b_v", "c_x", "c_b", "c_c", "d_q", "d_k", "d_v",
          "z_a", "z_b", "z_c", "z_d", "m_g")
_WIDTHS = (FW, SW, KV, KV, CW, CW, CW, DW, DW, DW, FW, SW, CW, DW, 4 * D)
COL = dict(zip(_NAMES, np.cumsum((0,) + _WIDTHS[:-1]).tolist()))

RAW = 4
HL = 4
BANKS = 4

V_NORM, V_BMOD, V_CONV, V_SUBLN, V_C, V_CC, V_ROWS = 0, 16, 64, 82, 84, 92, 100
KINDS = ("b_q", "b_k", "d_q", "d_k")


def lam_init(layer):
    return 0.8 - 0.6 * math.exp(-0.3 * layer)


class Step:

    def __init__(self, kind, layer, *, branch=None, stream=None, part=None, g=None, kb=None, after=None,
                 turned=None, j=None, n=None, used=None, kt=None, gate=None, n_g=None, name=None, w=None,
                 toks=None, qk=None, root=None, t=None, q=None, k=None, j0=None, x_uses=None, i=None,
                 z=None, before=None, weighed=None, half=None):
        self.kind, self.layer = kind, layer
        self.tiles, self.mods, self.uses, self.first_tile, self.ahead = [], [], [], 0, 0
        self.branch, self.stream, self.part, self.g, self.kb = branch, stream, part, g, kb
        self.after, self.turned, self.weighed, self.before = after, turned, weighed, before
        self.j, self.n, self.used, self.kt, self.gate, self.n_g = j, n, used, kt, gate, n_g
        self.name, self.w, self.toks, self.qk, self.root = name, w, toks, qk, root
        self.t, self.q, self.k, self.j0, self.x_uses = t, q, k, j0, x_uses
        self.i, self.z, self.half = i, z, half


class Plan:

    def __init__(self):
        self.steps, self.raw, self.split_raw, self.last_use = [], [], [], []
        self.uses = self.groups = self.qk = self.roots = self.z = self.gates = self.mod_tiles = 0

    def add(self, kind, layer, sources=(), mods=(), uses=1, **kw):
        s = Step(kind, layer, **kw)
        s.uses = list(range(self.uses, self.uses + uses))
        self.uses += uses
        s.first_tile = len(self.split_raw)
        for i, src in enumerate(mods):
            s.mods.append(len(self.raw))
            last = i == len(mods) - 1
            self.raw.append((src, None, ("use", s.uses[0]) if last else ("tile", self.mod_tiles + 1)))
            self.mod_tiles += not last
        for i, src in enumerate(sources):
            s.tiles.append(len(self.split_raw))
            self.split_raw.append(len(self.raw))
            self.raw.append((src, s.tiles[-1], None))
            self.last_use.append(s.uses[i] if kind == "conv" else s.uses[-1])
        self.steps.append(s)
        return s

    def look_ahead(self):
        barrier = len(self.raw) + RAW
        for s in reversed(self.steps):
            s.ahead = min(s.first_tile + HL, sum(n < barrier for n in self.split_raw))
            if s.mods:
                barrier = s.mods[0] + RAW

    def attention(self, branch, layer):
        after = self.uses
        groups = []
        for stream in range(2 if layer == 0 else 1):
            for part in range(4):
                groups.append(dict(branch=branch, stream=stream, part=part, g=self.groups,
                                   kb=4 if stream == 0 else 2, after=after))
                self.groups += 1
        turns = 4 if branch == "b" else 2
        periods = []
        for i in range(len(groups) + 1):
            micro = []
            if i:
                micro.append(("turn", turns, groups[i - 1]))
            if i < len(groups):
                micro.append(("score", 0, groups[i]))
            if i:
                micro.append(("weigh", 1, groups[i - 1]))
            periods.append(micro)
        return periods


def make_plan():
    p = Plan()
    turn_use = {}

    def w_in(layer, col):
        return ("w_in", layer, col, KD)

    def merge_phase(layer, branch, index, periods):
        n_g = p.z
        merges = []
        for j in range(KD):
            for k in range(len(periods) * j // KD, len(periods) * (j + 1) // KD):
                for kind, uses, group in periods[k]:
                    s = p.add(kind, layer, uses=uses, **group)
                    if kind == "turn":
                        turn_use[s.g] = s.uses[-1]
                    if kind == "score":
                        s.turned = turn_use.get(s.g - 1)
                    if kind == "weigh":
                        s.after = turn_use[s.g] + 1
            s = p.add("gate", layer, [w_in(layer, COL["m_g"] + index * D + j * P)], j=j,
                      n=p.gates, used=merges[-2] if j >= 2 else None)
            p.gates += 1
            kt = 3 if branch in "ac" else 4
            m = p.add("merge", layer, [("w_o_" + branch, layer, j * P, kt)], j=j, kt=kt,
                      branch=branch, n=s.n, gate=s.uses[0], n_g=n_g)
            merges.append(m.uses[0])

    def tokens(layer, name, w, src, toks, waiting):
        s = p.add("tokens", layer, src, uses=len(toks), name=name, w=w, toks=toks, qk=p.qk,
                  root=p.roots)
        if name != "d_v":
            p.qk += len(toks)
            p.roots += len(toks)
        for t in waiting:
            p.add("turn_qk", layer, **t)
        if name == "d_v":
            return []
        return [dict(name=name, w=w, t=t, q=s.qk + i) for i, t in enumerate(toks)]

    p.add("rows", 0, uses=3)
    for k in range(KD):
        p.add("turn_x", 0, k=k)
    p.add("mod", 0, mods=[("w_mod", 0, j * P, KD) for j in range(16)], j0=0, n=16)
    x_uses = None
    for layer in range(DEPTH):
        both = layer == 0
        p.add("norm", layer, uses=2, root=p.roots, after=p.uses, x_uses=x_uses)
        p.roots += 1
        waiting = []
        for name in ("d_q", "d_k", "d_v"):
            toks = list(range(4 if both or name != "d_q" else 2))
            for w in range(2):
                c0 = COL[name] + 2 * P * w
                waiting = tokens(layer, name, w, [w_in(layer, c0), w_in(layer, c0 + P)], toks, waiting)
        for i in range(3):
            p.add("conv", layer, [w_in(layer, COL[x] + i * P) for x in ("c_x", "c_c", "c_b", "z_c")],
                  uses=4, i=i, z=p.z, before=p.steps[-1].uses[1] if i else None)
            p.z += 1
        merge_phase(layer, "c", 2, p.attention("d", layer))
        p.add("d_norm", layer, uses=4 if both else 2, root=p.roots)
        p.roots += 4 if both else 2
        waiting = []
        for w in range(3):
            toks = list(range(4 if both or w == 2 else 2))
            if w < 2:
                src = [("heads", layer, COL["b_q"] + (2 * w + i) * HD, KD) for i in range(2)]
            else:
                src = [w_in(layer, COL["b_k"]), w_in(layer, COL["b_v"])]
            waiting = tokens(layer, "b_q" if w < 2 else "b_k", w, src, toks, waiting)
        for i in range(4):
            p.add("silu", layer, [w_in(layer, COL["z_d"] + i * P)], i=i, z=p.z)
            p.z += 1
            if i == 1:
                for t in waiting:
                    p.add("turn_qk", layer, **t)
        merge_phase(layer, "d", 3, p.attention("b", layer))
        weighed = [s for s in p.steps if s.kind == "weigh"][-1].uses[0]
        for i in range(4):
            p.add("silu", layer, [w_in(layer, COL["z_b"] + i * P)], i=i, z=p.z)
            p.z += 1
        for i in range(3):
            p.add("fourier_in", layer, [w_in(layer, COL["a_x"] + i * P)],
                  uses=4 if both else 2, i=i, weighed=weighed)
        after = p.uses
        merge_phase(layer, "b", 1, [])
        for s in range(2 if both else 1):
            for i in range(3):
                p.add("fourier_seq", layer, stream=s, i=i, after=after)
        after = p.uses
        for i in range(3):
            p.add("fourier_dim", layer, i=i, after=after)
        for i in range(3):
            p.add("silu", layer, [w_in(layer, COL["z_a"] + i * P)], i=i, z=p.z)
            p.z += 1
        merge_phase(layer, "a", 0, [])
        p.add("mod", layer, mods=[("w_mod", layer, j * P, KD) for j in range(16, 24)], j0=16, n=8)
        if both:
            p.add("mod", 1, mods=[("w_mod", 1, j * P, KD) for j in range(16)], j0=0, n=16)
        x_uses = []
        for j in range(KD):
            s = p.add("out", layer, [("w_out", layer, j * P, KD)], j=j)
            x_uses.append(s.uses[0])
    after = p.uses
    for t in range(2):
        for half in range(2):
            p.add("turn_out", 1, t=t, half=half, after=after)
    p.look_ahead()
    return p


def hybrid_backbone(nc, a, c, out):
    plan = make_plan()
    steps = plan.steps
    with ExitStack() as ctx:
        def sb(name, shape, dt=F32):
            return ctx.enter_context(nc.sbuf_tensor(name, shape, dt))

        def sem(name):
            return ctx.enter_context(nc.semaphore(name))

        xT = sb("xT", [P, KD, TOK])
        h_hi = sb("h_hi", [P, KD, TOK], F32R)
        h_lo = sb("h_lo", [P, KD, TOK], F32R)
        mixed = sb("mixed", [P, KD, TOK])
        w_raw = sb("w_raw", [P, RAW, KD, P])
        w_hi = sb("w_hi", [P, HL, KD, P], F32R)
        w_lo = sb("w_lo", [P, HL, KD, P], F32R)
        qkv = sb("qkv", [P, 3, 4, TOK])
        y = sb("y", [P, 4, TOK])
        o_d = sb("o_d", [P, 4, TOK])
        g_hi = sb("g_hi", [P, 4, TOK], F32R)
        g_lo = sb("g_lo", [P, 4, TOK], F32R)
        prob = sb("prob", [P, 4, TOK])
        probT = sb("probT", [P, 2, 4, 256])
        gate_t = sb("gate_t", [P, 2, TOK])
        tA = sb("tA", [P, TOK])
        tB = sb("tB", [P, TOK])
        tC = sb("tC", [P, TOK])
        ident = sb("ident", [P, P])
        ones = sb("ones", [P, P])
        dft_dim = sb("dft_dim", [P, 2, P])
        rope = sb("rope", [P, 2, 2, HD])
        rope_g = sb("rope_g", [P, 4, 2, 2, HD])
        masks = sb("masks", [P, 2, P])
        vec = sb("vec", [P, V_ROWS])
        gains = sb("gains", [P, DEPTH, 4, HD])
        tail = sb("tail", [P, 18])
        c_th = sb("c_th", [P, 16])
        sil = sb("sil", [P, KD, 2])
        modv = sb("modv", [P, 24, 2])
        amp = sb("amp", [P, KD, 2])
        gatev = sb("gatev", [P, KD, 2])
        ms = sb("ms", [P, 2, 4])
        rms = sb("rms", [P, 2, 4])
        minus_half = sb("minus_half", [P, 4])
        sm = sb("sm", [P, 32])
        sub_g = sb("sub_g", [P, DEPTH])
        lam_tmp = sb("lam_tmp", [1, 8])
        top, low, negmax, sink_d, sums, sink_e, inv, lam_inv = (sm[:, 4 * i:4 * i + 4] for i in range(8))

        qT, kT, v_tok = qkv[:, 0], qkv[:, 1], qkv[:, 2]
        x_in = qkv[:, 0:2].rearrange("p a b t -> p (a b t)").rearrange("p (t d) -> p t d", d=D)
        sq_x = qkv[:, 0:2].rearrange("p a b t -> p (a b) t")
        vec_rows = prob[0:V_ROWS, 0, 0:P]
        row = prob[0:1, 1:3].rearrange("p a t -> p (a t)")
        lam_rows = probT[0:1, 0, 0:2].rearrange("p a t -> p (a t)").rearrange("p (i l e) -> p i l e", i=4, l=2)
        diag = tA[:].rearrange("p (t q) -> p t q", t=4)
        conv_x = probT[:, 0, 0:2].rearrange("p a t -> p (a t)")
        conv_u = prob[:, 0:2].rearrange("p a t -> p (a t)")[:, 0:2 * 258].rearrange("p (s t) -> p s t", s=2)
        qn = o_d[:, 0:2].rearrange("p a t -> p (a t)").rearrange("p (r n) -> p r n", n=256)
        sq, th = gate_t[:, 0], gate_t[:, 1]
        dft_seq = probT[:, 0].rearrange("p k t -> p (k t)").rearrange("p (a n) -> p a n", a=2)
        u_a = qT
        f_seq = qkv[:, 1:3].rearrange("p a b t -> p (a b) t")

        score_ps = ctx.enter_context(nc.psum_tensor("score_ps", [P, 4, TOK], F32))
        work_ps = ctx.enter_context(nc.psum_tensor("work_ps", [P, BANKS, TOK], F32))

        raw_landed = [sem(f"raw_landed{i}") for i in range(RAW)]
        bank_full = [sem(f"bank_full{i}") for i in range(BANKS)]
        bank_free = [sem(f"bank_free{i}") for i in range(BANKS)]
        mod_read = sem("mod_read")
        hi_ready = sem("hi_ready")
        lo_ready = sem("lo_ready")
        x_landed = sem("x_landed")
        const_landed = sem("const_landed")
        dft_landed = sem("dft_landed")
        rows_landed = sem("rows_landed")
        ones_set = sem("ones_set")
        vec_ready = sem("vec_ready")
        c_tanh = sem("c_tanh")
        sil_ready = sem("sil_ready")
        lam_sums = sem("lam_sums")
        lam_exp = sem("lam_exp")
        lam_ready = sem("lam_ready")
        squares = sem("squares")
        half_set = sem("half_set")
        ms_ready = sem("ms_ready")
        rms_ready = sem("rms_ready")
        diag_ready = sem("diag_ready")
        mod_ready = sem("mod_ready")
        scaled = sem("scaled")
        modulated = sem("modulated")
        h_hi_ready = sem("h_hi_ready")
        h_lo_ready = sem("h_lo_ready")
        sq_ready = sem("sq_ready")
        qn_ready = sem("qn_ready")
        scores_done = sem("scores_done")
        negmax_ready = sem("negmax_ready")
        exp_done = sem("exp_done")
        prob_ready = sem("prob_ready")
        o_clamped = sem("o_clamped")
        o_normed = sem("o_normed")
        tanh_ready = sem("tanh_ready")
        gated = sem("gated")
        g_hi_ready = sem("g_hi_ready")
        g_lo_ready = sem("g_lo_ready")
        mixed_ready = sem("mixed_ready")
        row_out = sem("row_out")
        stored = sem("stored")
        dve_own = sem("dve_own")

        def full(eng, use):
            eng.wait_ge(bank_full[use % BANKS], use // BANKS + 1)

        def moved(eng, use):
            eng.wait_ge(bank_free[use % BANKS], use // BANKS + 1)

        def all_moved(eng, upto):
            for use in range(max(0, upto - BANKS), upto):
                moved(eng, use)

        def bank(use):
            return work_ps[:, use % BANKS]

        def streams(layer):
            return 2 if layer == 0 else 1

        def wide(s):
            return slice(SEQ * s, SEQ * (s + 1))

        def source(src):
            name, layer, col, kt = src
            w = a["w_in" if name == "heads" else name][layer].rearrange("(k p) n -> p k n", p=P)
            if name == "heads":
                return [(w[:, :, col:col + HD], 0, HD), (w[:, :, col + 4 * HD:col + 5 * HD], HD, HD)]
            return [(w[:, :, col:col + P], 0, P)]

        landed_at, per_slot = [], [0] * RAW
        for n, (src, _, _) in enumerate(plan.raw):
            per_slot[n % RAW] += 16 * len(source(src))
            landed_at.append(per_slot[n % RAW])

        def raw_wait(eng, n):
            eng.wait_ge(raw_landed[n % RAW], landed_at[n])

        dft_before = {plan.split_raw[s.tiles[0]]: s.weighed for s in steps if s.kind == "fourier_in" and s.i == 0}
        turn_of = {s.q: s.uses[0] for s in steps if s.kind == "turn_qk"}

        block = ctx.enter_context(nc.Block())

        @block.sync
        def _(sp):
            for t in range(4):
                src = a["x"][0] if t < 2 else a["ctx"][0]
                sp.dma_start(x_in[:, t], src[(t % 2) * P:(t % 2 + 1) * P, :]).then_inc(x_landed, 16)
            for n, (src, m, _) in enumerate(plan.raw):
                if n >= RAW:
                    _, m_old, read = plan.raw[n - RAW]
                    if m_old is not None:
                        sp.wait_ge(lo_ready, m_old + 1)
                    elif read[0] == "use":
                        full(sp, read[1])
                    else:
                        sp.wait_ge(mod_read, read[1])
                if n in dft_before:
                    full(sp, dft_before[n])
                    sp.dma_start(dft_seq, c["dft_seq"]).then_inc(dft_landed, 16)
                for ap, c0, w in source(src):
                    sp.dma_start(w_raw[:, n % RAW, 0:src[3], c0:c0 + w], ap).then_inc(raw_landed[n % RAW], 16)
            for i in range(4):
                sp.wait_ge(row_out, i + 1)
                t, half = i // 2, i % 2
                sp.dma_start(out[0, t * P:(t + 1) * P, half * 512:(half + 1) * 512], prob[:, i]).then_inc(stored, 16)
            sp.wait_ge(stored, 64)

        @block.gpsimd
        def _(pool):
            nc.gpsimd.memset(minus_half[:], -0.5).then_inc(half_set, 1)
            pool.wait_ge(half_set, 1)
            for s in steps:
                if s.kind not in ("norm", "tokens", "d_norm") or (s.kind == "tokens" and s.name == "d_v"):
                    continue
                for i in range(1 if s.kind == "norm" else len(s.uses)):
                    r = s.root + i
                    n = 2 if s.kind == "tokens" and s.name == "b_k" else 4
                    pool.wait_ge(ms_ready, r + 1)
                    nc.gpsimd.tensor_tensor(rms[:, r % 2, 0:n], ms[:, r % 2, 0:n], minus_half[:, 0:n],
                                            ALU.pow).then_inc(rms_ready, 1)

        @block.tensor
        def _(pe):
            def claim(use):
                if use >= BANKS:
                    moved(pe, use - BANKS)

            def done(ins, use):
                ins.then_inc(bank_full[use % BANKS], 1)

            def project(use, out_ap, tiles, hi, lo, cols, kt, weights_move=False, h_wait=None):
                claim(use)
                for k in range(kt):
                    if h_wait is not None:
                        pe.wait_ge(h_lo_ready, h_wait + k + 1)
                    for i, (wp, hp) in enumerate(((w_hi, hi), (w_hi, lo), (w_lo, hi))):
                        m = tiles[0] % HL
                        h = hp[:, k, cols]
                        if weights_move:
                            lhs, rhs = h, wp[:, m:m + len(tiles), k, :]
                        else:
                            lhs, rhs = wp[:, m, k, :], h
                        last = nc.tensor.matmul(out_ap, lhs, rhs, start=(k == 0 and i == 0),
                                                stop=(k == kt - 1 and i == 2))
                done(last, use)

            first_h = [True] * DEPTH
            for s in steps:
                L, u = s.layer, s.uses
                W = SEQ * streams(L)
                if s.tiles and s.kind != "conv":
                    pe.wait_ge(lo_ready, s.tiles[-1] + 1)
                if s.kind == "rows":
                    pe.wait_ge(rows_landed, 16 * 19)
                    pe.wait_ge(const_landed, 16 * 4)
                    done(nc.tensor.transpose(bank(u[0])[:, 0:V_ROWS], vec_rows, ident[0:V_ROWS, 0:V_ROWS]), u[0])
                    pe.wait_ge(ones_set, 1)
                    done(nc.tensor.matmul(bank(u[1]), ones[0:1, :], row[:, 0:512], start=True, stop=True), u[1])
                    pe.wait_ge(lam_ready, 1)
                    done(nc.tensor.matmul(bank(u[2])[:, 0:18], ones[0:1, :], row[:, 512:530],
                                          start=True, stop=True), u[2])
                elif s.kind == "turn_x":
                    if s.k == 0:
                        pe.wait_ge(x_landed, 16 * 4)
                    claim(u[0])
                    for t in range(4):
                        last = nc.tensor.transpose(bank(u[0])[:, t * P:(t + 1) * P],
                                                   x_in[:, t, s.k * P:(s.k + 1) * P], ident[:])
                    done(last, u[0])
                elif s.kind == "mod":
                    pe.wait_ge(sil_ready, 1)
                    claim(u[0])
                    for i, n in enumerate(s.mods):
                        raw_wait(pe, n)
                        for k in range(KD):
                            last = nc.tensor.matmul(bank(u[0])[:, 2 * i:2 * i + 2], w_raw[:, n % RAW, k, :],
                                                    sil[:, k, :], start=(k == 0), stop=(k == KD - 1))
                        if i < len(s.mods) - 1:
                            last.then_inc(mod_read, 1)
                    done(last, u[0])
                elif s.kind == "norm":
                    pe.wait_ge(squares, KD * (L + 1))
                    claim(u[0])
                    for t in range(4):
                        for k in range(KD):
                            last = nc.tensor.matmul(bank(u[0])[:, t:t + 1], sq_x[:, k, t * P:(t + 1) * P],
                                                    ones[:, 0:1], start=(k == 0), stop=(k == KD - 1))
                    done(last, u[0])
                    claim(u[1])
                    pe.wait_ge(diag_ready, L + 1)
                    for t in range(4):
                        last = nc.tensor.matmul(bank(u[1])[:, t * P:(t + 1) * P], ones[:], diag[:, t],
                                                start=True, stop=True)
                    done(last, u[1])
                elif s.kind in ("tokens", "fourier_in"):
                    n = P * len(s.tiles)
                    for t, use in enumerate(u):
                        wait = 2 * KD * L if first_h[L] else None
                        first_h[L] = False
                        project(use, bank(use)[:, 0:n], s.tiles, h_hi, h_lo, slice(t * P, (t + 1) * P),
                                KD, True, wait)
                elif s.kind == "turn_qk":
                    claim(u[0])
                    pe.wait_ge(qn_ready, s.q + 1)
                    for i in range(1 if s.name == "b_k" else 2):
                        last = nc.tensor.transpose(bank(u[0])[:, i * P:(i + 1) * P],
                                                   qn[:, s.q % 4, i * P:(i + 1) * P], ident[:])
                    done(last, u[0])
                elif s.kind in ("silu", "conv", "gate"):
                    for m, use in zip(s.tiles, u):
                        if s.kind == "conv":
                            pe.wait_ge(lo_ready, m + 1)
                        project(use, bank(use)[:, 0:W], [m], h_hi, h_lo, slice(0, W), KD)
                elif s.kind == "merge":
                    pe.wait_ge(g_lo_ready, s.n_g)
                    project(u[0], bank(u[0])[:, 0:W], s.tiles, g_hi, g_lo, slice(0, W), s.kt)
                elif s.kind == "out":
                    project(u[0], bank(u[0])[:, 0:W], s.tiles, h_hi, h_lo, slice(0, W), KD,
                            h_wait=2 * KD * L + KD if s.j == 0 else None)
                elif s.kind == "score":
                    if s.g:
                        pe.wait_ge(exp_done, s.g)
                    all_moved(pe, s.after)
                    k0, k1 = (0, TOK) if s.stream == 0 else (SEQ, TOK)
                    for i in range(4):
                        e, t = i // 2, i % 2
                        if s.branch == "d":
                            r, q, k = e, qT[:, s.part], kT[:, s.part]
                        else:
                            head = 2 * s.part + e
                            r, q, k = head // 4, qT[:, head % 4], kT[:, 0]
                        q0 = s.stream * SEQ + t * P
                        last = nc.tensor.matmul(score_ps[:, i, 0:k1 - k0], q[r * HD:(r + 1) * HD, q0:q0 + P],
                                                k[r * HD:(r + 1) * HD, k0:k1], start=True, stop=True)
                    last.then_inc(scores_done, 1)
                elif s.kind == "turn":
                    pe.wait_ge(prob_ready, s.g + 1)
                    for i, use in enumerate(u):
                        claim(use)
                        for kb in range(s.kb):
                            last = nc.tensor.transpose(bank(use)[:, kb * P:(kb + 1) * P],
                                                       prob[:, i, kb * P:(kb + 1) * P], ident[:])
                        done(last, use)
                elif s.kind == "weigh":
                    all_moved(pe, s.after)
                    claim(u[0])
                    tb = 0 if s.stream == 0 else 2
                    if s.branch == "b":
                        kv = s.part // 2
                        for e in range(2):
                            for kb in range(s.kb):
                                last = nc.tensor.matmul(
                                    bank(u[0])[e * HD:(e + 1) * HD, 0:256],
                                    v_tok[:, tb + kb, kv * HD:(kv + 1) * HD], probT[:, e, kb, :],
                                    start=(kb == 0), stop=(kb == s.kb - 1))
                    else:
                        for t in range(2):
                            for kb in range(s.kb):
                                last = nc.tensor.matmul(
                                    bank(u[0])[:, t * P:(t + 1) * P], probT[:, 0, kb, t * P:(t + 1) * P],
                                    v_tok[:, tb + kb, s.part * P:(s.part + 1) * P],
                                    start=(kb == 0), stop=(kb == s.kb - 1))
                    done(last, u[0])
                elif s.kind == "d_norm":
                    for t, use in enumerate(u):
                        claim(use)
                        pe.wait_ge(o_normed, (4 if L else 0) + t + 1)
                        for i in range(4):
                            last = nc.tensor.transpose(bank(use)[:, i * P:(i + 1) * P],
                                                       o_d[:, t, i * P:(i + 1) * P], ident[:])
                        done(last, use)
                elif s.kind == "fourier_seq":
                    all_moved(pe, s.after)
                    pe.wait_ge(dft_landed, 16 * (L + 1))
                    claim(u[0])
                    for t in range(2):
                        last = nc.tensor.matmul(bank(u[0]), u_a[:, 2 * s.stream + t, s.i * P:(s.i + 1) * P],
                                                dft_seq[:, t, :], start=(t == 0), stop=(t == 1))
                    done(last, u[0])
                elif s.kind == "fourier_dim":
                    all_moved(pe, s.after)
                    claim(u[0])
                    for st in range(streams(L)):
                        for part in range(2):
                            last = nc.tensor.matmul(bank(u[0])[:, wide(st)], dft_dim[:, part],
                                                    f_seq[:, 3 * st + s.i, part * SEQ:(part + 1) * SEQ],
                                                    start=(part == 0), stop=(part == 1))
                    done(last, u[0])
                elif s.kind == "turn_out":
                    all_moved(pe, s.after)
                    claim(u[0])
                    for i in range(4):
                        last = nc.tensor.transpose(bank(u[0])[:, i * P:(i + 1) * P],
                                                   xT[:, 4 * s.half + i, s.t * P:(s.t + 1) * P], ident[:])
                    done(last, u[0])

        @block.scalar
        def _(act):
            counts, last = {}, []

            def tick(ins, signal):
                counts[id(signal)] = counts.get(id(signal), 0) + 1
                ins.then_inc(signal, 1)
                last[:] = [signal, counts[id(signal)]]

            def free(ins, use):
                ins.then_inc(bank_free[use % BANKS], 1)
                last[:] = [bank_free[use % BANKS], use // BANKS + 1]

            def settle():
                if last:
                    act.wait_ge(*last)

            split = [0]

            def split_hi(upto):
                while split[0] < min(upto, len(plan.split_raw)):
                    m = split[0]
                    n = plan.split_raw[m]
                    kt = plan.raw[n][0][3]
                    raw_wait(act, n)
                    if m >= HL:
                        full(act, plan.last_use[m - HL])
                    tick(nc.scalar.activation(w_hi[:, m % HL, 0:kt], w_raw[:, n % RAW, 0:kt], ACT.Copy), hi_ready)
                    split[0] += 1

            for ap, name in ((ident, "ident"), (dft_dim, "dft_dim"),
                             (rope, "rope"), (masks, "masks")):
                act.dma_start(ap[:], c[name]).then_inc(const_landed, 16)
            loads = [(vec_rows[V_NORM:V_NORM + 16], a["norm_g"].rearrange("l (r p) -> (l r) p", p=P)),
                     (vec_rows[V_BMOD:V_BMOD + 48], a["b_mod"].rearrange("l (r p) -> (l r) p", p=P)),
                     (vec_rows[V_CONV:V_CONV + 18], a["conv_w"].rearrange("l k (r p) -> (l k r) p", p=P)),
                     (vec_rows[V_SUBLN:V_SUBLN + 2], a["subln_d"]),
                     (vec_rows[V_C:V_C + 8], a["c"].rearrange("b (r p) -> (b r) p", p=P)),
                     (vec_rows[V_CC:V_CC + 8], a["c_ctx"].rearrange("(r p) -> r p", p=P)),
                     (row[:, 512:528], a["sink_b"].rearrange("(o l) h -> o (l h)", o=1))]
            for i, name in enumerate(("q_norm_b", "k_norm_b", "q_norm_d", "k_norm_d")):
                for L in range(DEPTH):
                    c0 = (L * 4 + i) * HD
                    loads.append((row[:, c0:c0 + HD], a[name][L:L + 1, :]))
            for i, name in enumerate(("lam_q1", "lam_k1", "lam_q2", "lam_k2")):
                loads.append((lam_rows[:, i], a[name].rearrange("(o l) e -> o l e", o=1)))
            for ap, src in loads:
                act.dma_start(ap, src).then_inc(rows_landed, 16)

            def z_gate(s, use):
                W = SEQ * streams(s.layer)
                all_moved(act, s.uses[0])
                full(act, use)
                tick(nc.scalar.activation(th[:, 0:W], bank(use)[:, 0:W], ACT.Tanh, scale=0.5), tanh_ready)
                act.wait_ge(gated, s.z + 1)
                tick(nc.scalar.activation(g_hi[:, s.i, 0:W], tC[:, 0:W], ACT.Copy), g_hi_ready)

            for s in steps:
                L, u = s.layer, s.uses
                settle()
                W = SEQ * streams(L)
                split_hi(s.ahead)
                if s.kind == "rows":
                    act.wait_ge(lam_sums, 1)
                    tick(nc.scalar.activation(lam_tmp[:, 4:8], lam_tmp[:, 0:4], ACT.Exp), lam_exp)
                    act.wait_ge(vec_ready, 1)
                    tick(nc.scalar.activation(c_th[:], vec[:, V_C:V_C + 16], ACT.Tanh, scale=0.5), c_tanh)
                elif s.kind == "turn_x":
                    full(act, u[0])
                    free(nc.scalar.activation(xT[:, s.k], bank(u[0]), ACT.Copy), u[0])
                elif s.kind == "norm":
                    for k in range(KD):
                        if L == 0:
                            all_moved(act, s.after)
                        else:
                            moved(act, s.x_uses[k])
                        tick(nc.scalar.activation(sq_x[:, k], xT[:, k], ACT.Square), squares)
                    act.wait_ge(mod_ready, L + 1)
                    for k in range(KD):
                        act.wait_ge(scaled, KD * L + k + 1)
                        for st in range(2):
                            tick(nc.scalar.activation(mixed[:, k, wide(st)], mixed[:, k, wide(st)], ACT.Identity,
                                                 scale=amp[:, k, st:st + 1],
                                                 bias=modv[:, k, st:st + 1]), modulated)
                        act.wait_ge(modulated, 2 * (KD * L + k + 1))
                        tick(nc.scalar.activation(h_hi[:, k], mixed[:, k], ACT.Copy), h_hi_ready)
                elif s.kind == "tokens":
                    for i, (use, t) in enumerate(zip(u, s.toks)):
                        full(act, use)
                        if s.name == "d_v":
                            free(nc.scalar.activation(v_tok[:, t, s.w * 256:(s.w + 1) * 256],
                                                      bank(use)[:, 0:256], ACT.Copy), use)
                            continue
                        if s.name == "b_k":
                            nc.scalar.activation(v_tok[:, t, 0:P], bank(use)[:, P:2 * P], ACT.Copy)
                        n = P if s.name == "b_k" else 256
                        act.wait_ge(ms_ready, s.root + i)
                        tick(nc.scalar.activation(sq[:, 0:n], bank(use)[:, 0:n], ACT.Square), sq_ready)
                elif s.kind == "turn_qk":
                    full(act, u[0])
                    tok = slice(s.t * P, (s.t + 1) * P)
                    if s.name == "b_k":
                        free(nc.scalar.activation(kT[:, 0, tok], bank(u[0])[:, 0:P], ACT.Copy), u[0])
                    else:
                        to = (kT if s.name == "d_k" else qT)[:, 2 * s.w:2 * s.w + 2, tok]
                        free(nc.scalar.activation(to, bank(u[0])[:, 0:256].rearrange("p (a t) -> p a t", a=2),
                                                  ACT.Copy), u[0])
                elif s.kind == "conv":
                    full(act, u[0])
                    if s.before is not None:
                        moved(act, s.before)
                    free(nc.scalar.activation(conv_x[:, 0:W], bank(u[0])[:, 0:W], ACT.Copy), u[0])
                    for i in range(1, 4):
                        split_hi(s.first_tile + HL + i)
                    z_gate(s, u[3])
                elif s.kind == "silu":
                    z_gate(s, u[0])
                elif s.kind == "gate":
                    full(act, u[0])
                    if s.used is not None:
                        moved(act, s.used)
                    free(nc.scalar.activation(gate_t[:, s.n % 2, 0:W], bank(u[0])[:, 0:W], ACT.Tanh, scale=0.5), u[0])
                elif s.kind == "score":
                    nk = s.kb * P
                    act.wait_ge(negmax_ready, s.g + 1)
                    if s.turned is not None:
                        full(act, s.turned)
                    for i in range(4):
                        ins = nc.scalar.activation(prob[:, i, 0:nk], score_ps[:, i, 0:nk], ACT.Exp, scale=SCALE,
                                                   bias=negmax[:, i:i + 1], accum_out=sums[:, i:i + 1])
                    if s.branch == "b":
                        ins = nc.scalar.activation(sink_e, sink_d, ACT.Exp)
                    tick(ins, exp_done)
                elif s.kind == "turn":
                    for i, use in enumerate(u):
                        if i % 2 == 0:
                            full(act, use)
                            e, t = (i // 2, i % 2) if s.branch == "b" else (0, i)
                            free(nc.scalar.activation(
                                probT[:, e, 0:s.kb, t * P:(t + 1) * P],
                                bank(use)[:, 0:s.kb * P].rearrange("p (k q) -> p k q", k=s.kb), ACT.Copy), use)
                elif s.kind == "weigh":
                    full(act, u[0])
                    if s.branch == "b":
                        free(nc.scalar.activation(y[:, s.part, wide(s.stream)], bank(u[0])[:, 0:256], ACT.Copy), u[0])
                    else:
                        free(nc.scalar.activation(
                            o_d[:, 2 * s.stream:2 * s.stream + 2, s.part * P:(s.part + 1) * P],
                            bank(u[0])[:, 0:256].rearrange("p (t e) -> p t e", t=2), ACT.Copy), u[0])
                elif s.kind == "d_norm":
                    all_moved(act, u[0])
                    for t in range(len(u)):
                        act.wait_ge(ms_ready, s.root + t)
                        act.wait_ge(o_clamped, (4 if L else 0) + t + 1)
                        tick(nc.scalar.activation(sq, (tB, tC)[t % 2][:], ACT.Square, scale=1.0 / BIG ** 0.5), sq_ready)
                    for t, use in enumerate(u):
                        full(act, use)
                        free(nc.scalar.activation(y[:, :, t * P:(t + 1) * P],
                                                  bank(use).rearrange("p (i q) -> p i q", i=4),
                                                  ACT.Copy, scale=sub_g[:, L:L + 1]), use)
                elif s.kind == "fourier_in":
                    for t, use in enumerate(u):
                        full(act, use)
                        free(nc.scalar.activation(u_a[:, t, s.i * P:(s.i + 1) * P], bank(use)[:, 0:P], ACT.Copy), use)
                elif s.kind == "fourier_seq":
                    full(act, u[0])
                    free(nc.scalar.activation(f_seq[:, 3 * s.stream + s.i], bank(u[0]), ACT.Copy), u[0])
                elif s.kind == "fourier_dim":
                    full(act, u[0])
                    free(nc.scalar.activation(y[:, s.i, 0:W], bank(u[0])[:, 0:W], ACT.Copy), u[0])
                elif s.kind == "merge" and s.branch == "a" and s.j == KD - 1:
                    full(act, u[0])
                    for k in range(KD):
                        act.wait_ge(mixed_ready, KD * L + k + 1)
                        tick(nc.scalar.activation(h_hi[:, k, 0:W], mixed[:, k, 0:W], ACT.Copy), h_hi_ready)
                elif s.kind == "turn_out":
                    full(act, u[0])
                    tick(nc.scalar.activation(prob[:, 2 * s.t + s.half], bank(u[0]), ACT.Copy), row_out)

        @block.vector
        def _(dve):
            counts, last = {}, []

            def tick(ins, signal):
                counts[id(signal)] = counts.get(id(signal), 0) + 1
                ins.then_inc(signal, 1)
                last[:] = [signal, counts[id(signal)]]

            def free(ins, use):
                ins.then_inc(bank_free[use % BANKS], 1)
                last[:] = [bank_free[use % BANKS], use // BANKS + 1]

            def settle():
                if last:
                    dve.wait_ge(*last)

            def link(ins):
                tick(ins, dve_own)
                settle()

            split = [0]

            def split_lo(upto):
                while split[0] < min(upto, len(plan.split_raw)):
                    m = split[0]
                    n = plan.split_raw[m]
                    kt = plan.raw[n][0][3]
                    dve.wait_ge(hi_ready, m + 1)
                    tick(nc.vector.tensor_tensor(w_lo[:, m % HL, 0:kt], w_raw[:, n % RAW, 0:kt],
                                            w_hi[:, m % HL, 0:kt].bitcast(F32), ALU.subtract), lo_ready)
                    split[0] += 1

            def h_lo_part(k, count, W):
                dve.wait_ge(h_hi_ready, count)
                tick(nc.vector.tensor_tensor(h_lo[:, k, 0:W], mixed[:, k, 0:W], h_hi[:, k, 0:W].bitcast(F32),
                                        ALU.subtract), h_lo_ready)

            def z_gate(s, use, y_ap):
                W = SEQ * streams(s.layer)
                dve.wait_ge(tanh_ready, s.z + 1)
                ins = nc.vector.scalar_tensor_tensor(tB[:, 0:W], th[:, 0:W], 1.0, bank(use)[:, 0:W], ALU.add, ALU.mult)
                free(ins, use)
                moved(dve, use)
                tick(nc.vector.tensor_tensor(tC[:, 0:W], tB[:, 0:W], y_ap, ALU.mult), gated)
                dve.wait_ge(g_hi_ready, s.z + 1)
                tick(nc.vector.tensor_tensor(g_lo[:, s.i, 0:W], tC[:, 0:W], g_hi[:, s.i, 0:W].bitcast(F32),
                                        ALU.subtract), g_lo_ready)

            waiting = []

            def normalise():
                if not waiting:
                    return
                s = waiting.pop()
                nk = s.kb * P
                dve.wait_ge(exp_done, s.g + 1)
                if s.branch == "b":
                    link(nc.vector.tensor_tensor(sums, sums, sink_e, ALU.add))
                link(nc.vector.reciprocal(inv, sums))
                if s.branch == "b":
                    for i in range(4):
                        ins = nc.vector.tensor_scalar(prob[:, i, 0:nk], prob[:, i, 0:nk], inv[:, i:i + 1], None, ALU.mult)
                else:
                    minus_lam = tail[:, 16 + s.layer:17 + s.layer]
                    nc.vector.tensor_scalar(lam_inv[:, 0:2], inv[:, 2:4], minus_lam, None, ALU.mult)
                    for t in range(2):
                        ins = nc.vector.tensor_scalar(prob[:, t, 0:nk], prob[:, t, 0:nk], inv[:, t:t + 1], None, ALU.mult)
                    link(ins)
                    for t in range(2):
                        ins = nc.vector.scalar_tensor_tensor(prob[:, t, 0:nk], prob[:, 2 + t, 0:nk],
                                                             lam_inv[:, t:t + 1], prob[:, t, 0:nk], ALU.mult, ALU.add)
                tick(ins, prob_ready)

            tick(nc.vector.memset(ones[:], 1.0), ones_set)
            for s in steps:
                L, u = s.layer, s.uses
                settle()
                S = streams(L)
                W = SEQ * S
                split_lo(s.ahead)
                if s.kind in ("turn", "merge", "d_norm", "silu"):
                    normalise()
                if s.kind == "rows":
                    dve.wait_ge(rows_landed, 16 * 19)
                    lam_v = lam_rows.rearrange("p (a b) l e -> p a b l e", b=2)
                    for i in range(2):
                        ins = nc.vector.tensor_tensor(tA[0:1, 128 * i:128 * i + 128].rearrange("p (l e) -> p l e", l=2),
                                                      lam_v[:, i, 0], lam_v[:, i, 1], ALU.mult)
                    link(ins)
                    tick(nc.vector.tensor_reduce(lam_tmp[:, 0:4], tA[0:1, 0:256].rearrange("p (g e) -> p g e", g=4),
                                            AX.X, ALU.add), lam_sums)
                    dve.wait_ge(lam_exp, 1)
                    link(nc.vector.tensor_tensor(lam_tmp[:, 0:2], lam_tmp[:, 6:8], lam_tmp[:, 4:6], ALU.subtract))
                    for layer in range(DEPTH):
                        ins = nc.vector.tensor_scalar(row[:, 528 + layer:529 + layer], lam_tmp[:, layer:layer + 1],
                                                      -lam_init(layer), None, ALU.add)
                    tick(ins, lam_ready)
                    full(dve, u[0])
                    free(nc.vector.tensor_copy(vec[:], bank(u[0])[:, 0:V_ROWS]), u[0])
                    full(dve, u[1])
                    free(nc.vector.tensor_copy(gains[:].rearrange("p l k e -> p (l k e)"), bank(u[1])), u[1])
                    full(dve, u[2])
                    free(nc.vector.tensor_copy(tail[:], bank(u[2])[:, 0:18]), u[2])
                    moved(dve, u[0])
                    for layer in range(DEPTH):
                        tick(nc.vector.tensor_scalar(sub_g[:, layer:layer + 1], vec[:, V_SUBLN + layer:V_SUBLN + layer + 1],
                                                1.0 - lam_init(layer), None, ALU.mult), vec_ready)
                    dve.wait_ge(c_tanh, 1)
                    tick(nc.vector.scalar_tensor_tensor(sil[:].rearrange("p k s -> p s k"),
                                                   c_th[:].rearrange("p (s k) -> p s k", s=2), 1.0,
                                                   vec[:, V_C:V_C + 16].rearrange("p (s k) -> p s k", s=2),
                                                   ALU.add, ALU.mult), sil_ready)
                elif s.kind == "mod":
                    full(dve, u[0])
                    bias = vec[:, V_BMOD + 24 * L + s.j0:V_BMOD + 24 * L + s.j0 + s.n]
                    ins = nc.vector.scalar_tensor_tensor(
                        modv[:, s.j0:s.j0 + s.n, :], bank(u[0])[:, 0:2 * s.n].rearrange("p (j s) -> p j s", s=2), 0.5,
                        bias.unsqueeze(2).to_broadcast([P, s.n, 2]), ALU.mult, ALU.add)
                    free(ins, u[0])
                    moved(dve, u[0])
                    if s.j0 == 0:
                        g = vec[:, V_NORM + KD * L:V_NORM + KD * (L + 1)]
                        tick(nc.vector.scalar_tensor_tensor(amp[:], modv[:, KD:2 * KD, :], 1.0,
                                                       g.unsqueeze(2).to_broadcast([P, KD, 2]),
                                                       ALU.add, ALU.mult), mod_ready)
                    else:
                        link(nc.vector.tensor_scalar(gatev[:], modv[:, 2 * KD:3 * KD, :], 0.25, None, ALU.mult))
                elif s.kind == "norm":
                    if L == 0:
                        dve.wait_ge(const_landed, 16 * 4)
                        moved(dve, 1)
                    for kd in range(4):
                        gain = gains[:, L, kd]
                        nc.vector.tensor_tensor(rope_g[:, kd, 0], rope[:, 0],
                                                gain.unsqueeze(1).to_broadcast([P, 2, HD]), ALU.mult)
                        to = rope_g[:, kd, 1].rearrange("p t (g s e) -> p t g s e", g=2, s=2)
                        sn = rope[:, 1].rearrange("p t (g s e) -> p t g s e", g=2, s=2)
                        gv = gain.rearrange("p (g s e) -> p g s e", g=2, s=2)
                        for h in range(2):
                            ins = nc.vector.tensor_tensor(to[:, :, :, h], sn[:, :, :, h],
                                                          gv[:, :, 1 - h].unsqueeze(1).to_broadcast([P, 2, 2, 16]),
                                                          ALU.mult)
                    link(ins)
                    full(dve, u[0])
                    r = s.root
                    ins = nc.vector.tensor_scalar(ms[:, r % 2], bank(u[0])[:, 0:4], 1.0 / D, EPS, ALU.mult, ALU.add)
                    tick(ins, ms_ready)
                    dve.wait_ge(rms_ready, r + 1)
                    free(nc.vector.tensor_copy(tB[:, 0:4], bank(u[0])[:, 0:4]), u[0])
                    for t in range(4):
                        ins = nc.vector.tensor_scalar(diag[:, t], ident[:], rms[:, r % 2, t:t + 1], None, ALU.mult)
                    tick(ins, diag_ready)
                    full(dve, u[1])
                    for k in range(KD):
                        ins = nc.vector.tensor_tensor(mixed[:, k], xT[:, k], bank(u[1]), ALU.mult)
                        tick(ins, scaled)
                        if k:
                            h_lo_part(k - 1, 2 * KD * L + k, TOK)
                    h_lo_part(KD - 1, 2 * KD * L + KD, TOK)
                    free(nc.vector.tensor_copy(tB[:, 0:4], bank(u[1])[:, 0:4]), u[1])
                elif s.kind == "tokens" and s.name != "d_v":
                    nh = 2 if s.name == "b_k" else 4
                    n = nh * HD
                    kd = KINDS.index(s.name)
                    for i, (use, t) in enumerate(zip(u, s.toks)):
                        q, r = s.qk + i, s.root + i
                        dve.wait_ge(sq_ready, r - L)
                        link(nc.vector.tensor_reduce(tA[:, 0:nh], sq[:, 0:n].rearrange("p (h e) -> p h e", e=HD),
                                                     AX.X, ALU.add))
                        tick(nc.vector.tensor_scalar(ms[:, r % 2, 0:nh], tA[:, 0:nh], 1.0 / HD, EPS,
                                                ALU.mult, ALU.add), ms_ready)
                        ps = bank(use)[:, 0:n].rearrange("p (h e) -> p h e", e=HD)
                        tb = tB[:, 0:n].rearrange("p (h e) -> p h e", e=HD)
                        if t < 2:
                            nc.vector.tensor_tensor(tb, ps, rope_g[:, kd, 0, t].unsqueeze(1).to_broadcast([P, nh, HD]),
                                                    ALU.mult)
                            p5 = bank(use)[:, 0:n].rearrange("p (h g s e) -> p h g s e", g=2, s=2, e=16)
                            t5 = tC[:, 0:n].rearrange("p (h g s e) -> p h g s e", g=2, s=2, e=16)
                            sn = rope_g[:, kd, 1, t].rearrange("p (g s e) -> p g s e", g=2, s=2)
                            for h in range(2):
                                ins = nc.vector.tensor_tensor(t5[:, :, :, h], p5[:, :, :, 1 - h],
                                                              sn[:, :, h].unsqueeze(1).to_broadcast([P, nh, 2, 16]),
                                                              ALU.mult)
                            free(ins, use)
                            moved(dve, use)
                            link(nc.vector.tensor_tensor(tB[:, 0:n], tB[:, 0:n], tC[:, 0:n], ALU.add))
                        else:
                            free(nc.vector.tensor_tensor(tb, ps, gains[:, L, kd].unsqueeze(1).to_broadcast([P, nh, HD]),
                                                         ALU.mult), use)
                            moved(dve, use)
                        dve.wait_ge(rms_ready, r + 1)
                        if q >= 4:
                            full(dve, turn_of[q - 4])
                        tick(nc.vector.tensor_tensor(qn[:, q % 4, 0:n].rearrange("p (h e) -> p h e", e=HD), tb,
                                                rms[:, r % 2, 0:nh].unsqueeze(2).to_broadcast([P, nh, HD]),
                                                ALU.mult), qn_ready)
                elif s.kind == "conv":
                    full(dve, u[1])
                    cu = conv_u[:, 0:S]
                    if s.i == 0:
                        nc.vector.memset(conv_u[:, :, 0:1], 0.0)
                        nc.vector.memset(conv_u[:, :, 257:258], 0.0)
                    moved(dve, u[0])
                    free(nc.vector.tensor_tensor(cu[:, :, 1:257], conv_x[:, 0:W].rearrange("p (s t) -> p s t", s=S),
                                                 bank(u[1])[:, 0:W].rearrange("p (s t) -> p s t", s=S), ALU.mult), u[1])
                    moved(dve, u[1])
                    ta = tA[:, 0:W].rearrange("p (s t) -> p s t", s=S)
                    tap = [vec[:, V_CONV + 9 * L + 3 * j + s.i:V_CONV + 9 * L + 3 * j + s.i + 1] for j in range(3)]
                    link(nc.vector.tensor_scalar(ta, cu[:, :, 0:256], tap[0], None, ALU.mult))
                    for j in (1, 2):
                        link(nc.vector.scalar_tensor_tensor(ta, cu[:, :, j:j + 256], tap[j], ta, ALU.mult, ALU.add))
                    split_lo(s.first_tile + HL + 1)
                    full(dve, u[2])
                    free(nc.vector.tensor_tensor(tA[:, 0:W], tA[:, 0:W], bank(u[2])[:, 0:W], ALU.mult), u[2])
                    moved(dve, u[2])
                    split_lo(s.first_tile + HL + 3)
                    z_gate(s, u[3], tA[:, 0:W])
                elif s.kind == "silu":
                    all_moved(dve, u[0])
                    z_gate(s, u[0], y[:, s.i, 0:W])
                elif s.kind == "merge":
                    full(dve, u[0])
                    moved(dve, s.gate)
                    gate = gate_t[:, s.n % 2, 0:W]
                    if s.branch == "c":
                        free(nc.vector.scalar_tensor_tensor(mixed[:, s.j, 0:W], gate, 1.0, bank(u[0])[:, 0:W],
                                                            ALU.add, ALU.mult), u[0])
                    else:
                        free(nc.vector.scalar_tensor_tensor(tB[:, 0:W], gate, 1.0, bank(u[0])[:, 0:W],
                                                            ALU.add, ALU.mult), u[0])
                        moved(dve, u[0])
                        ins = nc.vector.tensor_tensor(mixed[:, s.j, 0:W], mixed[:, s.j, 0:W], tB[:, 0:W], ALU.add)
                        tick(ins, mixed_ready if s.branch == "a" else dve_own)
                        if s.branch == "a":
                            if s.j == KD - 1:
                                for k in range(KD):
                                    h_lo_part(k, 2 * KD * L + KD + k + 1, W)
                elif s.kind == "out":
                    full(dve, u[0])
                    for st in range(S):
                        ins = nc.vector.scalar_tensor_tensor(xT[:, s.j, wide(st)], bank(u[0])[:, wide(st)],
                                                             gatev[:, s.j, st:st + 1], xT[:, s.j, wide(st)],
                                                             ALU.mult, ALU.add)
                    free(ins, u[0])
                elif s.kind == "score":
                    nk = s.kb * P
                    dve.wait_ge(scores_done, s.g + 1)
                    if s.branch == "b" and s.stream == 0:
                        sv = score_ps[:].rearrange("p (e t) k -> p e t k", e=2)
                        for t, c0 in ((0, P), (1, 0)):
                            o = sv[:, :, t, c0:c0 + P]
                            ins = nc.vector.tensor_tensor(o, o, masks[:, t].unsqueeze(1).to_broadcast([P, 2, P]), ALU.add)
                        link(ins)
                    link(nc.vector.tensor_reduce(top, score_ps[:, :, 0:nk], AX.X, ALU.max))
                    if s.branch == "b":
                        c0 = 8 * L + 2 * s.part
                        sink = tail[:, c0:c0 + 2].unsqueeze(2).to_broadcast([P, 2, 2])
                        low_v = low.rearrange("p (e t) -> p e t", e=2)
                        link(nc.vector.scalar_tensor_tensor(low_v, top.rearrange("p (e t) -> p e t", e=2), SCALE, sink,
                                                            ALU.mult, ALU.max))
                        nc.vector.tensor_tensor(sink_d.rearrange("p (e t) -> p e t", e=2), sink, low_v, ALU.subtract)
                        tick(nc.vector.tensor_scalar(negmax, low, -1.0, None, ALU.mult), negmax_ready)
                    else:
                        tick(nc.vector.tensor_scalar(negmax, top, -SCALE, None, ALU.mult), negmax_ready)
                    waiting.append(s)
                elif s.kind == "turn":
                    for i, use in enumerate(u):
                        if i % 2:
                            full(dve, use)
                            e, t = (i // 2, i % 2) if s.branch == "b" else (0, i)
                            free(nc.vector.tensor_copy(
                                probT[:, e, 0:s.kb, t * P:(t + 1) * P],
                                bank(use)[:, 0:s.kb * P].rearrange("p (k q) -> p k q", k=s.kb)), use)
                elif s.kind == "d_norm":
                    def clamp(t):
                        tick(nc.vector.tensor_scalar((tB, tC)[t % 2][:], o_d[:, t], BIG, -BIG, ALU.min, ALU.max),
                             o_clamped)

                    all_moved(dve, u[0])
                    clamp(0)
                    for t in range(len(u)):
                        r = s.root + t
                        dve.wait_ge(sq_ready, r - L)
                        if t + 1 < len(u):
                            clamp(t + 1)
                            settle()
                        link(nc.vector.tensor_reduce(tA[:, 0:4], sq.rearrange("p (h e) -> p h e", e=P),
                                                     AX.X, ALU.add))
                        link(nc.vector.tensor_scalar(tA[:, 4:8], tA[:, 0:4], BIG, BIG / P, ALU.min, ALU.mult))
                        tick(nc.vector.tensor_scalar(ms[:, r % 2], tA[:, 4:8], EPS, None, ALU.add), ms_ready)
                        dve.wait_ge(rms_ready, r + 1)
                        link(nc.vector.scalar_tensor_tensor(tA[:, 8:12], tA[:, 0:4], BIG, rms[:, r % 2],
                                                            ALU.is_lt, ALU.mult))
                        o = o_d[:, t].rearrange("p (h e) -> p h e", e=P)
                        tick(nc.vector.tensor_tensor(o, o, tA[:, 8:12].unsqueeze(2).to_broadcast([P, 4, P]),
                                                     ALU.mult), o_normed)


def constants():
    n = np.arange(SEQ)
    seq = 2 * np.pi * ((n[:, None] * n[None, :]) % SEQ) / SEQ
    cs = np.concatenate([np.cos(seq), np.sin(seq)], axis=1).astype(np.float32)
    d = np.arange(HD)
    dim = 2 * np.pi * ((d[:, None] * d[None, :]) % HD) / HD
    norm = 1.0 / math.sqrt(SEQ * HD)
    dft_dim = np.stack([np.kron(np.eye(2), np.cos(dim) * norm), np.kron(np.eye(2), -np.sin(dim) * norm)], axis=1)
    nf = HD // 4
    freq = np.float32(10000.0) ** (-np.arange(nf, dtype=np.float32) / np.float32(nf))
    ar = (n // GRID_W).astype(np.float32)[:, None] * freq[None, :]
    ac = (n % GRID_W).astype(np.float32)[:, None] * freq[None, :]
    cos = np.concatenate([np.cos(ar), np.cos(ar), np.cos(ac), np.cos(ac)], axis=1)
    sin = np.concatenate([-np.sin(ar), np.sin(ar), -np.sin(ac), np.sin(ac)], axis=1)
    rope = np.stack([cos, sin]).reshape(2, 2, P, HD).transpose(2, 0, 1, 3)
    q = np.arange(P)[:, None]
    k = np.arange(P)[None, :]
    masks = np.stack([np.where(k + P - q <= WINDOW, 0.0, MASKED), np.where(q + P - k <= WINDOW, 0.0, MASKED)], axis=1)
    return {
        "ident": np.eye(P, dtype=np.float32),
        "dft_seq": np.ascontiguousarray(cs.reshape(2, P, 2 * SEQ).transpose(1, 0, 2)),
        "dft_dim": np.ascontiguousarray(dft_dim.astype(np.float32)),
        "rope": np.ascontiguousarray(rope.astype(np.float32)),
        "masks": np.ascontiguousarray(masks.astype(np.float32)),
    }


_INS = ["x", "c", "ctx", "c_ctx", "norm_g", "w_mod", "b_mod", "w_in", "q_norm_b", "k_norm_b", "sink_b",
        "conv_w", "q_norm_d", "k_norm_d", "lam_q1", "lam_k1", "lam_q2", "lam_k2", "subln_d",
        "w_o_a", "w_o_b", "w_o_c", "w_o_d", "w_out"]


def kernel(**inputs):
    import concourse.bacc as bacc
    from concourse.bass_utils import run_bass_kernel_spmd

    nc = bacc.Bacc("TRN2", target_bir_lowering=False, num_devices=1)
    arrays, ins, consts = {}, {}, {}
    for name in _INS:
        v = np.ascontiguousarray(inputs[name])
        arrays[f"in_{name}"] = v
        ins[name] = nc.dram_tensor(f"in_{name}", v.shape, mybir.dt.from_np(v.dtype), kind="ExternalInput").ap()
    for name, v in constants().items():
        arrays[f"const_{name}"] = v
        consts[name] = nc.dram_tensor(f"const_{name}", v.shape, mybir.dt.from_np(v.dtype), kind="ExternalInput").ap()
    out = nc.dram_tensor("out_0", (1, SEQ, D), F32, kind="ExternalOutput").ap()
    hybrid_backbone(nc, ins, consts, out)
    r = run_bass_kernel_spmd(nc, [arrays], core_ids=[0])
    return r.results[0]["out_0"]
```

```python
import math
from contextlib import ExitStack

import numpy as np

import concourse.bass as bass
from concourse import mybir

F32 = mybir.dt.float32
F32R = mybir.dt.float32r
ALU = mybir.AluOpType
ACT = mybir.ActivationFunctionType
AX = mybir.AxisListType

P = 128
D = 1024
KD = D // P
SEQ = 256
CTX = 256
TOK = SEQ + CTX
DEPTH = 2
GRID_W = 64
HD = 64
FW, SW, KV, CW, DW = 384, 512, 128, 384, 512
WINDOW = 128
EPS = 1e-6
SCALE = HD ** -0.5
MASKED = -1e30
BIG = 2.0 ** 64

_NAMES = ("a_x", "b_q", "b_k", "b_v", "c_x", "c_b", "c_c", "d_q", "d_k", "d_v",
          "z_a", "z_b", "z_c", "z_d", "m_g")
_WIDTHS = (FW, SW, KV, KV, CW, CW, CW, DW, DW, DW, FW, SW, CW, DW, 4 * D)
COL = dict(zip(_NAMES, np.cumsum((0,) + _WIDTHS[:-1]).tolist()))

RAW = 4
HL = 4
BANKS = 4

V_NORM, V_BMOD, V_CONV, V_SUBLN, V_C, V_CC, V_ROWS = 0, 16, 64, 82, 84, 92, 100
KINDS = ("b_q", "b_k", "d_q", "d_k")


def lam_init(layer):
    return 0.8 - 0.6 * math.exp(-0.3 * layer)


class Step:

    def __init__(self, kind, layer, *, branch=None, stream=None, part=None, g=None, kb=None, after=None,
                 turned=None, j=None, n=None, used=None, kt=None, gate=None, n_g=None, name=None, w=None,
                 toks=None, qk=None, root=None, t=None, q=None, k=None, j0=None, x_uses=None, i=None,
                 z=None, before=None, weighed=None, half=None):
        self.kind, self.layer = kind, layer
        self.tiles, self.uses, self.first_tile = [], [], 0
        self.branch, self.stream, self.part, self.g, self.kb = branch, stream, part, g, kb
        self.after, self.turned, self.weighed, self.before = after, turned, weighed, before
        self.j, self.n, self.used, self.kt, self.gate, self.n_g = j, n, used, kt, gate, n_g
        self.name, self.w, self.toks, self.qk, self.root = name, w, toks, qk, root
        self.t, self.q, self.k, self.j0, self.x_uses = t, q, k, j0, x_uses
        self.i, self.z, self.half = i, z, half


class Plan:

    def __init__(self):
        self.steps, self.tiles, self.last_use = [], [], []
        self.uses = self.groups = self.qk = self.roots = self.z = self.gates = self.normed = 0

    def add(self, kind, layer, sources=(), uses=1, **kw):
        s = Step(kind, layer, **kw)
        s.uses = list(range(self.uses, self.uses + uses))
        self.uses += uses
        s.first_tile = len(self.tiles)
        for i, src in enumerate(sources):
            s.tiles.append(len(self.tiles))
            self.tiles.append(src)
            self.last_use.append(s.uses[i] if kind == "conv" else s.uses[-1])
        self.steps.append(s)
        return s

    def attention(self, branch, layer):
        after = self.uses
        groups = []
        for stream in range(2 if layer == 0 else 1):
            for part in range(4):
                groups.append(dict(branch=branch, stream=stream, part=part, g=self.groups,
                                   kb=4 if stream == 0 else 2, after=after))
                self.groups += 1
        turns = 4 if branch == "b" else 2
        periods = []
        for i in range(len(groups) + 1):
            micro = []
            if i:
                micro.append(("turn", turns, groups[i - 1]))
            if i < len(groups):
                micro.append(("score", 0, groups[i]))
            if i:
                micro.append(("weigh", 1, groups[i - 1]))
            periods.append(micro)
        return periods


def make_plan():
    p = Plan()
    turn_use = {}

    def w_in(layer, col):
        return ("w_in", layer, col, KD)

    def merge_phase(layer, branch, index, periods):
        n_g = p.z
        merges = []
        for j in range(KD + 1):
            lo, hi = (len(periods) - 1) * j // KD, (len(periods) - 1) * (j + 1) // KD
            if layer:
                lo, hi = (j // 2, j // 2 + 1) if j % 2 == 0 else (0, 0)
            elif j == KD:
                hi = len(periods)
            for period in periods[lo:hi] if periods else []:
                for kind, uses, group in period:
                    s = p.add(kind, layer, uses=uses, **group)
                    if kind == "turn":
                        turn_use[s.g] = s.uses[-1]
                    if kind == "score":
                        s.turned = turn_use.get(s.g - 1)
                    if kind == "weigh":
                        s.after = turn_use[s.g] + 1
            if j == KD:
                break
            s = p.add("gate", layer, [w_in(layer, COL["m_g"] + index * D + j * P)], j=j,
                      n=p.gates, used=merges[-2] if j >= 2 else None)
            p.gates += 1
            kt = 3 if branch in "ac" else 4
            m = p.add("merge", layer, [("w_o_" + branch, layer, j * P, kt)], j=j, kt=kt,
                      branch=branch, n=s.n, gate=s.uses[0], n_g=n_g)
            merges.append(m.uses[0])

    waiting = []

    def turn_waiting(layer, left, in_use=None):
        while len(waiting) > left:
            s = p.add("turn_qk", layer, **waiting.pop(0))
            if in_use is not None:
                s.first_tile = in_use

    def tokens(layer, name, w, src, toks):
        first = len(p.tiles)
        for t in toks:
            last = p.uses
            s = p.add("tokens", layer, src if t == toks[0] else [], name=name, w=w, t=t, qk=p.qk, root=p.roots)
            s.tiles, s.first_tile = [first, first + 1], first
            if name != "d_v":
                waiting.append(dict(name=name, w=w, t=t, q=p.qk))
                p.qk += 1
                p.roots += 1
            turn_waiting(layer, 2, first if t != toks[-1] else None)
        p.last_use[first] = p.last_use[first + 1] = last

    def modulation(layer, j0, n):
        for w in range(n // 2):
            p.add("mod", layer, [("w_mod", layer, (j0 + 2 * w + i) * P, KD) for i in range(2)], w=w)
        p.add("mod_turn", layer, j0=j0, n=n)

    p.add("rows", 0, uses=3)
    for k in range(KD):
        p.add("turn_x", 0, k=k)
    modulation(0, 0, 16)
    x_uses = None
    for layer in range(DEPTH):
        both = layer == 0
        p.add("norm", layer, uses=2, root=p.roots, after=p.uses, x_uses=x_uses)
        p.roots += 1
        for name in ("d_q", "d_k", "d_v"):
            toks = list(range(4 if both or name != "d_q" else 2))
            for w in range(2):
                c0 = COL[name] + 2 * P * w
                tokens(layer, name, w, [w_in(layer, c0), w_in(layer, c0 + P)], toks)
        turn_waiting(layer, 0)
        for i in range(3):
            p.add("conv", layer, [w_in(layer, COL[x] + i * P) for x in ("c_x", "c_c", "c_b", "z_c")],
                  uses=4, i=i, z=p.z, before=p.steps[-1].uses[1] if i else None)
            p.z += 1
        merge_phase(layer, "c", 2, p.attention("d", layer))

        def d_root(toks):
            p.add("d_root", layer, uses=0, toks=toks, root=p.roots, n=p.normed, after=p.uses)
            p.roots += len(toks)
            p.normed += len(toks)
            return [dict(t=t, n=p.normed - len(toks) + i) for i, t in enumerate(toks)]

        turns = d_root([0, 1])
        for w in range(3):
            toks = list(range(4 if both or w == 2 else 2))
            if w < 2:
                src = [("heads", layer, COL["b_q"] + (2 * w + i) * HD, KD) for i in range(2)]
            else:
                src = [w_in(layer, COL["b_k"]), w_in(layer, COL["b_v"])]
            tokens(layer, "b_q" if w < 2 else "b_k", w, src, toks)
            for t in turns:
                p.add("d_turn", layer, **t)
            turns = d_root([2, 3]) if both and w == 0 else []
        for i in range(4):
            p.add("silu", layer, [w_in(layer, COL["z_d"] + i * P)], i=i, z=p.z)
            p.z += 1
            turn_waiting(layer, 0)
        merge_phase(layer, "d", 3, p.attention("b", layer))
        weighed = [s for s in p.steps if s.kind == "weigh"][-1].uses[0]
        for i in range(4):
            if i == 2:
                assert len(p.tiles) % HL == 0
                p.add("fourier_in", layer, [w_in(layer, COL["a_x"] + n * P) for n in range(3)],
                      uses=4 if both else 2, weighed=weighed)
            p.add("silu", layer, [w_in(layer, COL["z_b"] + i * P)], i=i, z=p.z)
            p.z += 1
        after = p.uses
        merge_phase(layer, "b", 1, [])
        for s in range(2 if both else 1):
            for i in range(3):
                p.add("fourier_seq", layer, stream=s, i=i, after=after)
        after = p.uses
        for i in range(3):
            p.add("fourier_dim", layer, i=i, after=after)
        for i in range(3):
            p.add("silu", layer, [w_in(layer, COL["z_a"] + i * P)], i=i, z=p.z)
            p.z += 1
        merge_phase(layer, "a", 0, [])
        modulation(layer, 16, 8)
        if both:
            modulation(1, 0, 16)
        x_uses = []
        for j in range(KD):
            s = p.add("out", layer, [("w_out", layer, j * P, KD)], j=j)
            x_uses.append(s.uses[0])
    after = p.uses
    for t in range(2):
        for half in range(2):
            p.add("turn_out", 1, t=t, half=half, after=after)
    return p


def hybrid_backbone(nc, a, c, out):
    plan = make_plan()
    steps = plan.steps
    with ExitStack() as ctx:
        def sb(name, shape, dt=F32):
            return ctx.enter_context(nc.sbuf_tensor(name, shape, dt))

        def sem(name):
            return ctx.enter_context(nc.semaphore(name))

        xT = sb("xT", [P, KD, TOK])
        h_hi = sb("h_hi", [P, KD, TOK], F32R)
        h_lo = sb("h_lo", [P, KD, TOK], F32R)
        mixed = sb("mixed", [P, KD, TOK])
        w_raw = sb("w_raw", [P, RAW, KD, P])
        w_hi = sb("w_hi", [P, HL, KD, P], F32R)
        w_lo = sb("w_lo", [P, HL, KD, P], F32R)
        qkv = sb("qkv", [P, 3, 4, TOK])
        y = sb("y", [P, 4, TOK])
        o_d = sb("o_d", [P, 4, TOK])
        g_hi = sb("g_hi", [P, 4, TOK], F32R)
        g_lo = sb("g_lo", [P, 4, TOK], F32R)
        prob = sb("prob", [P, 4, TOK])
        probT = sb("probT", [P, 2, 4, 256])
        gate_t = sb("gate_t", [P, 2, TOK])
        tA = sb("tA", [P, TOK])
        tB = sb("tB", [P, TOK])
        tC = sb("tC", [P, TOK])
        ident = sb("ident", [P, P])
        ones = sb("ones", [P, P])
        dft_dim = sb("dft_dim", [P, 2, P])
        rope = sb("rope", [P, 2, 2, HD])
        rope_g = sb("rope_g", [P, 4, 2, 2, HD])
        masks = sb("masks", [P, 2, P])
        vec = sb("vec", [P, V_ROWS])
        gains = sb("gains", [P, DEPTH, 4, HD])
        tail = sb("tail", [P, 18])
        c_th = sb("c_th", [P, 16])
        sil = sb("sil", [P, KD, 2])
        sil4 = sb("sil4", [P, KD, 4], F32R)
        modv = sb("modv", [P, 24, 2])
        amp = sb("amp", [P, KD, 2])
        gatev = sb("gatev", [P, KD, 2])
        ms = sb("ms", [P, 2, 4])
        rms = sb("rms", [P, 2, 4])
        minus_half = sb("minus_half", [P, 4])
        sm = sb("sm", [P, 32])
        sub_g = sb("sub_g", [P, DEPTH])
        lam_tmp = sb("lam_tmp", [1, 8])
        top, low, negmax, sink_d, sums, sink_e, inv, lam_inv = (sm[:, 4 * i:4 * i + 4] for i in range(8))

        qT, kT, v_tok = qkv[:, 0], qkv[:, 1], qkv[:, 2]
        x_in = qkv[:, 0:2].rearrange("p a b t -> p (a b t)").rearrange("p (t d) -> p t d", d=D)
        sq_x = qkv[:, 0:2].rearrange("p a b t -> p (a b) t")
        vec_rows = prob[0:V_ROWS, 0, 0:P]
        row = prob[0:1, 1:3].rearrange("p a t -> p (a t)")
        lam_rows = probT[0:1, 0, 0:2].rearrange("p a t -> p (a t)").rearrange("p (i l e) -> p i l e", i=4, l=2)
        mod_rows = prob[0:4].rearrange("p a t -> p (a t)")
        diag = tA[:].rearrange("p (t q) -> p t q", t=4)
        conv_x = probT[:, 0, 0:2].rearrange("p a t -> p (a t)")
        conv_u = prob[:, 0:2].rearrange("p a t -> p (a t)")[:, 0:2 * 258].rearrange("p (s t) -> p s t", s=2)
        qn = prob[:, 2:4].rearrange("p a t -> p (a t)").rearrange("p (r n) -> p r n", n=256)
        sq, th = gate_t[:, 0], gate_t[:, 1]
        dft_seq = probT[:, 0].rearrange("p k t -> p (k t)").rearrange("p (a n) -> p a n", a=2)
        u_a = qT
        f_seq = qkv[:, 1:3].rearrange("p a b t -> p (a b) t")

        score_ps = ctx.enter_context(nc.psum_tensor("score_ps", [P, 4, TOK], F32))
        work_ps = ctx.enter_context(nc.psum_tensor("work_ps", [P, BANKS, TOK], F32))

        raw_landed = [sem(f"raw_landed{i}") for i in range(RAW)]
        bank_full = [sem(f"bank_full{i}") for i in range(BANKS)]
        bank_free = [sem(f"bank_free{i}") for i in range(BANKS)]
        sq_summed = sem("sq_summed")
        hi_ready = sem("hi_ready")
        lo_ready = sem("lo_ready")
        x_landed = sem("x_landed")
        const_landed = sem("const_landed")
        dft_landed = sem("dft_landed")
        rows_landed = sem("rows_landed")
        ones_set = sem("ones_set")
        vec_ready = sem("vec_ready")
        c_tanh = sem("c_tanh")
        sil_ready = sem("sil_ready")
        lam_sums = sem("lam_sums")
        lam_exp = sem("lam_exp")
        lam_ready = sem("lam_ready")
        squares = sem("squares")
        half_set = sem("half_set")
        ms_ready = sem("ms_ready")
        rms_ready = sem("rms_ready")
        diag_ready = sem("diag_ready")
        mod_ready = sem("mod_ready")
        scaled = sem("scaled")
        modulated = sem("modulated")
        h_hi_ready = sem("h_hi_ready")
        h_lo_ready = sem("h_lo_ready")
        sq_ready = sem("sq_ready")
        qn_ready = sem("qn_ready")
        scores_done = sem("scores_done")
        negmax_ready = sem("negmax_ready")
        exp_done = sem("exp_done")
        prob_ready = sem("prob_ready")
        o_clamped = sem("o_clamped")
        o_normed = sem("o_normed")
        tanh_ready = sem("tanh_ready")
        gated = sem("gated")
        g_hi_ready = sem("g_hi_ready")
        g_lo_ready = sem("g_lo_ready")
        mixed_ready = sem("mixed_ready")
        row_out = sem("row_out")
        stored = sem("stored")
        dve_own = sem("dve_own")

        def full(eng, use):
            eng.wait_ge(bank_full[use % BANKS], use // BANKS + 1)

        def moved(eng, use):
            eng.wait_ge(bank_free[use % BANKS], use // BANKS + 1)

        def all_moved(eng, upto):
            for use in range(max(0, upto - BANKS), upto):
                moved(eng, use)

        def bank(use):
            return work_ps[:, use % BANKS]

        def streams(layer):
            return 2 if layer == 0 else 1

        def wide(s):
            return slice(SEQ * s, SEQ * (s + 1))

        def source(src):
            name, layer, col, kt = src
            w = a["w_in" if name == "heads" else name][layer].rearrange("(k p) n -> p k n", p=P)
            if name == "heads":
                return [(w[:, :, col:col + HD], 0, HD), (w[:, :, col + 4 * HD:col + 5 * HD], HD, HD)]
            return [(w[:, :, col:col + P], 0, P)]

        landed_at, per_slot = [], [0] * RAW
        for n, src in enumerate(plan.tiles):
            per_slot[n % RAW] += 16 * len(source(src))
            landed_at.append(per_slot[n % RAW])

        def raw_wait(eng, n):
            eng.wait_ge(raw_landed[n % RAW], landed_at[n])

        dft_before = {s.tiles[-1] + 1: s.weighed for s in steps if s.kind == "fourier_in"}
        turn_of = {s.q: s.uses[0] for s in steps if s.kind == "turn_qk"}

        block = ctx.enter_context(nc.Block())

        @block.sync
        def _(sp):
            for t in range(4):
                src = a["x"][0] if t < 2 else a["ctx"][0]
                sp.dma_start(x_in[:, t], src[(t % 2) * P:(t % 2 + 1) * P, :]).then_inc(x_landed, 16)
            for n, src in enumerate(plan.tiles):
                if n >= RAW:
                    sp.wait_ge(lo_ready, n - RAW + 1)
                if n in dft_before:
                    full(sp, dft_before[n])
                    sp.dma_start(dft_seq, c["dft_seq"]).then_inc(dft_landed, 16)
                for ap, c0, w in source(src):
                    sp.dma_start(w_raw[:, n % RAW, 0:src[3], c0:c0 + w], ap).then_inc(raw_landed[n % RAW], 16)
            for i in range(4):
                sp.wait_ge(row_out, i + 1)
                t, half = i // 2, i % 2
                sp.dma_start(out[0, t * P:(t + 1) * P, half * 512:(half + 1) * 512], prob[:, i]).then_inc(stored, 16)
            sp.wait_ge(stored, 64)

        @block.gpsimd
        def _(pool):
            nc.gpsimd.memset(minus_half[:], -0.5).then_inc(half_set, 1)
            pool.wait_ge(half_set, 1)
            for s in steps:
                if s.kind not in ("norm", "tokens", "d_root") or s.name == "d_v":
                    continue
                for i in range(len(s.toks) if s.kind == "d_root" else 1):
                    r = s.root + i
                    n = 2 if s.kind == "tokens" and s.name == "b_k" else 4
                    pool.wait_ge(ms_ready, r + 1)
                    nc.gpsimd.tensor_tensor(rms[:, r % 2, 0:n], ms[:, r % 2, 0:n], minus_half[:, 0:n],
                                            ALU.pow).then_inc(rms_ready, 1)

        @block.tensor
        def _(pe):
            def claim(use):
                if use >= BANKS:
                    moved(pe, use - BANKS)

            def done(ins, use):
                ins.then_inc(bank_full[use % BANKS], 1)

            def project(use, out_ap, tiles, hi, lo, cols, kt, weights_move=False, h_wait=None):
                claim(use)
                for k in range(kt):
                    if h_wait is not None:
                        pe.wait_ge(h_lo_ready, h_wait + k + 1)
                    for i, (wp, hp) in enumerate(((w_hi, hi), (w_hi, lo), (w_lo, hi))):
                        m = tiles[0] % HL
                        h = hp[:, k, cols]
                        if weights_move:
                            lhs, rhs = h, wp[:, m:m + len(tiles), k, :]
                        else:
                            lhs, rhs = wp[:, m, k, :], h
                        last = nc.tensor.matmul(out_ap, lhs, rhs, start=(k == 0 and i == 0),
                                                stop=(k == kt - 1 and i == 2))
                done(last, use)

            first_h = [True] * DEPTH
            for s in steps:
                L, u = s.layer, s.uses
                W = SEQ * streams(L)
                if s.tiles and s.kind != "conv":
                    pe.wait_ge(lo_ready, s.tiles[-1] + 1)
                if s.kind == "rows":
                    pe.wait_ge(rows_landed, 16 * 19)
                    pe.wait_ge(const_landed, 16 * 4)
                    done(nc.tensor.transpose(bank(u[0])[:, 0:V_ROWS], vec_rows, ident[0:V_ROWS, 0:V_ROWS]), u[0])
                    pe.wait_ge(ones_set, 1)
                    done(nc.tensor.matmul(bank(u[1]), ones[0:1, :], row[:, 0:512], start=True, stop=True), u[1])
                    pe.wait_ge(lam_ready, 1)
                    done(nc.tensor.matmul(bank(u[2])[:, 0:18], ones[0:1, :], row[:, 512:530],
                                          start=True, stop=True), u[2])
                elif s.kind == "turn_x":
                    if s.k == 0:
                        pe.wait_ge(x_landed, 16 * 4)
                    claim(u[0])
                    for t in range(4):
                        last = nc.tensor.transpose(bank(u[0])[:, t * P:(t + 1) * P],
                                                   x_in[:, t, s.k * P:(s.k + 1) * P], ident[:])
                    done(last, u[0])
                elif s.kind == "mod":
                    pe.wait_ge(sil_ready, 2)
                    claim(u[0])
                    m = s.tiles[0] % HL
                    for k in range(KD):
                        for w in (w_hi, w_lo):
                            last = nc.tensor.matmul(bank(u[0])[0:4, 0:256], sil4[:, k, :], w[:, m:m + 2, k, :],
                                                    start=(k == 0 and w is w_hi), stop=(k == KD - 1 and w is w_lo))
                    done(last, u[0])
                elif s.kind == "mod_turn":
                    all_moved(pe, u[0])
                    claim(u[0])
                    for i in range(s.n):
                        last = nc.tensor.transpose(bank(u[0])[:, 4 * i:4 * i + 4], mod_rows[:, i * P:(i + 1) * P],
                                                   ident[0:4, 0:4])
                    done(last, u[0])
                elif s.kind == "norm":
                    pe.wait_ge(sq_summed, L + 1)
                    claim(u[0])
                    for t in range(4):
                        last = nc.tensor.matmul(bank(u[0])[:, t:t + 1], sq_x[:, 0, t * P:(t + 1) * P],
                                                ones[:, 0:1], start=True, stop=True)
                    done(last, u[0])
                    claim(u[1])
                    pe.wait_ge(diag_ready, L + 1)
                    for t in range(4):
                        last = nc.tensor.matmul(bank(u[1])[:, t * P:(t + 1) * P], ones[:], diag[:, t],
                                                start=True, stop=True)
                    done(last, u[1])
                elif s.kind in ("tokens", "fourier_in"):
                    n = P * len(s.tiles)
                    for t, use in enumerate(u, s.t or 0):
                        wait = 2 * KD * L if first_h[L] else None
                        first_h[L] = False
                        project(use, bank(use)[:, 0:n], s.tiles, h_hi, h_lo, slice(t * P, (t + 1) * P),
                                KD, True, wait)
                elif s.kind == "turn_qk":
                    claim(u[0])
                    pe.wait_ge(qn_ready, s.q + 1)
                    for i in range(1 if s.name == "b_k" else 2):
                        last = nc.tensor.transpose(bank(u[0])[:, i * P:(i + 1) * P],
                                                   qn[:, s.q % 4, i * P:(i + 1) * P], ident[:])
                    done(last, u[0])
                elif s.kind in ("silu", "conv", "gate"):
                    for m, use in zip(s.tiles, u):
                        if s.kind == "conv":
                            pe.wait_ge(lo_ready, m + 1)
                        project(use, bank(use)[:, 0:W], [m], h_hi, h_lo, slice(0, W), KD)
                elif s.kind == "merge":
                    pe.wait_ge(g_lo_ready, s.n_g)
                    project(u[0], bank(u[0])[:, 0:W], s.tiles, g_hi, g_lo, slice(0, W), s.kt)
                elif s.kind == "out":
                    project(u[0], bank(u[0])[:, 0:W], s.tiles, h_hi, h_lo, slice(0, W), KD,
                            h_wait=2 * KD * L + KD if s.j == 0 else None)
                elif s.kind == "score":
                    if s.g:
                        pe.wait_ge(exp_done, s.g)
                    all_moved(pe, s.after)
                    k0, k1 = (0, TOK) if s.stream == 0 else (SEQ, TOK)
                    for i in range(4):
                        e, t = i // 2, i % 2
                        if s.branch == "d":
                            r, q, k = e, qT[:, s.part], kT[:, s.part]
                        else:
                            head = 2 * s.part + e
                            r, q, k = head // 4, qT[:, head % 4], kT[:, 0]
                        q0 = s.stream * SEQ + t * P
                        last = nc.tensor.matmul(score_ps[:, i, 0:k1 - k0], q[r * HD:(r + 1) * HD, q0:q0 + P],
                                                k[r * HD:(r + 1) * HD, k0:k1], start=True, stop=True)
                    last.then_inc(scores_done, 1)
                elif s.kind == "turn":
                    pe.wait_ge(prob_ready, s.g + 1)
                    for i, use in enumerate(u):
                        claim(use)
                        for kb in range(s.kb):
                            last = nc.tensor.transpose(bank(use)[:, kb * P:(kb + 1) * P],
                                                       prob[:, i, kb * P:(kb + 1) * P], ident[:])
                        done(last, use)
                elif s.kind == "weigh":
                    all_moved(pe, s.after)
                    claim(u[0])
                    tb = 0 if s.stream == 0 else 2
                    if s.branch == "b":
                        kv = s.part // 2
                        for e in range(2):
                            for kb in range(s.kb):
                                last = nc.tensor.matmul(
                                    bank(u[0])[e * HD:(e + 1) * HD, 0:256],
                                    v_tok[:, tb + kb, kv * HD:(kv + 1) * HD], probT[:, e, kb, :],
                                    start=(kb == 0), stop=(kb == s.kb - 1))
                    else:
                        for t in range(2):
                            for kb in range(s.kb):
                                last = nc.tensor.matmul(
                                    bank(u[0])[:, t * P:(t + 1) * P], probT[:, 0, kb, t * P:(t + 1) * P],
                                    v_tok[:, tb + kb, s.part * P:(s.part + 1) * P],
                                    start=(kb == 0), stop=(kb == s.kb - 1))
                    done(last, u[0])
                elif s.kind == "d_turn":
                    claim(u[0])
                    pe.wait_ge(o_normed, s.n + 1)
                    for i in range(4):
                        last = nc.tensor.transpose(bank(u[0])[:, i * P:(i + 1) * P],
                                                   o_d[:, s.t, i * P:(i + 1) * P], ident[:])
                    done(last, u[0])
                elif s.kind == "fourier_seq":
                    all_moved(pe, s.after)
                    pe.wait_ge(dft_landed, 16 * (L + 1))
                    claim(u[0])
                    for t in range(2):
                        last = nc.tensor.matmul(bank(u[0]), u_a[:, 2 * s.stream + t, s.i * P:(s.i + 1) * P],
                                                dft_seq[:, t, :], start=(t == 0), stop=(t == 1))
                    done(last, u[0])
                elif s.kind == "fourier_dim":
                    all_moved(pe, s.after)
                    claim(u[0])
                    for st in range(streams(L)):
                        for part in range(2):
                            last = nc.tensor.matmul(bank(u[0])[:, wide(st)], dft_dim[:, part],
                                                    f_seq[:, 3 * st + s.i, part * SEQ:(part + 1) * SEQ],
                                                    start=(part == 0), stop=(part == 1))
                    done(last, u[0])
                elif s.kind == "turn_out":
                    all_moved(pe, s.after)
                    claim(u[0])
                    for i in range(4):
                        last = nc.tensor.transpose(bank(u[0])[:, i * P:(i + 1) * P],
                                                   xT[:, 4 * s.half + i, s.t * P:(s.t + 1) * P], ident[:])
                    done(last, u[0])

        @block.scalar
        def _(act):
            counts, last = {}, []

            def tick(ins, signal):
                counts[id(signal)] = counts.get(id(signal), 0) + 1
                ins.then_inc(signal, 1)
                last[:] = [signal, counts[id(signal)]]

            def free(ins, use):
                ins.then_inc(bank_free[use % BANKS], 1)
                last[:] = [bank_free[use % BANKS], use // BANKS + 1]

            def settle():
                if last:
                    act.wait_ge(*last)

            split = [0]

            def split_hi(upto):
                while split[0] < min(upto, len(plan.tiles)):
                    m = split[0]
                    kt = plan.tiles[m][3]
                    raw_wait(act, m)
                    if m >= HL:
                        full(act, plan.last_use[m - HL])
                    tick(nc.scalar.activation(w_hi[:, m % HL, 0:kt], w_raw[:, m % RAW, 0:kt], ACT.Copy), hi_ready)
                    split[0] += 1

            for ap, name in ((ident, "ident"), (dft_dim, "dft_dim"),
                             (rope, "rope"), (masks, "masks")):
                act.dma_start(ap[:], c[name]).then_inc(const_landed, 16)
            loads = [(vec_rows[V_NORM:V_NORM + 16], a["norm_g"].rearrange("l (r p) -> (l r) p", p=P)),
                     (vec_rows[V_BMOD:V_BMOD + 48], a["b_mod"].rearrange("l (r p) -> (l r) p", p=P)),
                     (vec_rows[V_CONV:V_CONV + 18], a["conv_w"].rearrange("l k (r p) -> (l k r) p", p=P)),
                     (vec_rows[V_SUBLN:V_SUBLN + 2], a["subln_d"]),
                     (vec_rows[V_C:V_C + 8], a["c"].rearrange("b (r p) -> (b r) p", p=P)),
                     (vec_rows[V_CC:V_CC + 8], a["c_ctx"].rearrange("(r p) -> r p", p=P)),
                     (row[:, 512:528], a["sink_b"].rearrange("(o l) h -> o (l h)", o=1))]
            for i, name in enumerate(("q_norm_b", "k_norm_b", "q_norm_d", "k_norm_d")):
                for L in range(DEPTH):
                    c0 = (L * 4 + i) * HD
                    loads.append((row[:, c0:c0 + HD], a[name][L:L + 1, :]))
            for i, name in enumerate(("lam_q1", "lam_k1", "lam_q2", "lam_k2")):
                loads.append((lam_rows[:, i], a[name].rearrange("(o l) e -> o l e", o=1)))
            for ap, src in loads:
                act.dma_start(ap, src).then_inc(rows_landed, 16)

            def z_gate(s, use):
                W = SEQ * streams(s.layer)
                all_moved(act, s.uses[0])
                full(act, use)
                tick(nc.scalar.activation(th[:, 0:W], bank(use)[:, 0:W], ACT.Tanh, scale=0.5), tanh_ready)
                act.wait_ge(gated, s.z + 1)
                tick(nc.scalar.activation(g_hi[:, s.i, 0:W], tC[:, 0:W], ACT.Copy), g_hi_ready)

            for s in steps:
                L, u = s.layer, s.uses
                settle()
                W = SEQ * streams(L)
                split_hi(s.first_tile + HL)
                if s.kind == "rows":
                    act.wait_ge(lam_sums, 1)
                    tick(nc.scalar.activation(lam_tmp[:, 4:8], lam_tmp[:, 0:4], ACT.Exp), lam_exp)
                    act.wait_ge(vec_ready, 1)
                    tick(nc.scalar.activation(c_th[:], vec[:, V_C:V_C + 16], ACT.Tanh, scale=0.5), c_tanh)
                elif s.kind == "mod":
                    full(act, u[0])
                    free(nc.scalar.activation(mod_rows[:, 256 * s.w:256 * (s.w + 1)], bank(u[0])[0:4, 0:256],
                                              ACT.Copy), u[0])
                elif s.kind == "turn_x":
                    full(act, u[0])
                    free(nc.scalar.activation(xT[:, s.k], bank(u[0]), ACT.Copy), u[0])
                elif s.kind == "norm":
                    for k in range(0 if L == 0 else KD - 1, KD):
                        if L == 0:
                            all_moved(act, s.after)
                        else:
                            moved(act, s.x_uses[k])
                        tick(nc.scalar.activation(sq_x[:, k], xT[:, k], ACT.Square), squares)
                    act.wait_ge(mod_ready, L + 1)
                    for k in range(KD):
                        act.wait_ge(scaled, KD * L + k + 1)
                        for st in range(2):
                            tick(nc.scalar.activation(mixed[:, k, wide(st)], mixed[:, k, wide(st)], ACT.Identity,
                                                 scale=amp[:, k, st:st + 1],
                                                 bias=modv[:, k, st:st + 1]), modulated)
                        act.wait_ge(modulated, 2 * (KD * L + k + 1))
                        tick(nc.scalar.activation(h_hi[:, k], mixed[:, k], ACT.Copy), h_hi_ready)
                elif s.kind == "tokens":
                    for i, (use, t) in enumerate(((u[0], s.t),)):
                        full(act, use)
                        if s.name == "d_v":
                            free(nc.scalar.activation(v_tok[:, t, s.w * 256:(s.w + 1) * 256],
                                                      bank(use)[:, 0:256], ACT.Copy), use)
                            continue
                        if s.name == "b_k":
                            nc.scalar.activation(v_tok[:, t, 0:P], bank(use)[:, P:2 * P], ACT.Copy)
                        n = P if s.name == "b_k" else 256
                        act.wait_ge(ms_ready, s.root + i)
                        tick(nc.scalar.activation(sq[:, 0:n], bank(use)[:, 0:n], ACT.Square), sq_ready)
                elif s.kind == "turn_qk":
                    full(act, u[0])
                    tok = slice(s.t * P, (s.t + 1) * P)
                    if s.name == "b_k":
                        free(nc.scalar.activation(kT[:, 0, tok], bank(u[0])[:, 0:P], ACT.Copy), u[0])
                    else:
                        to = (kT if s.name == "d_k" else qT)[:, 2 * s.w:2 * s.w + 2, tok]
                        free(nc.scalar.activation(to, bank(u[0])[:, 0:256].rearrange("p (a t) -> p a t", a=2),
                                                  ACT.Copy), u[0])
                elif s.kind == "conv":
                    full(act, u[0])
                    if s.before is not None:
                        moved(act, s.before)
                    free(nc.scalar.activation(conv_x[:, 0:W], bank(u[0])[:, 0:W], ACT.Copy), u[0])
                    for i in range(1, 4):
                        split_hi(s.first_tile + HL + i)
                    z_gate(s, u[3])
                elif s.kind == "silu":
                    z_gate(s, u[0])
                elif s.kind == "gate":
                    full(act, u[0])
                    if s.used is not None:
                        moved(act, s.used)
                    free(nc.scalar.activation(gate_t[:, s.n % 2, 0:W], bank(u[0])[:, 0:W], ACT.Tanh, scale=0.5), u[0])
                elif s.kind == "score":
                    nk = s.kb * P
                    act.wait_ge(negmax_ready, s.g + 1)
                    if s.turned is not None:
                        full(act, s.turned)
                    for i in range(4):
                        ins = nc.scalar.activation(prob[:, i, 0:nk], score_ps[:, i, 0:nk], ACT.Exp, scale=SCALE,
                                                   bias=negmax[:, i:i + 1], accum_out=sums[:, i:i + 1])
                    if s.branch == "b":
                        ins = nc.scalar.activation(sink_e, sink_d, ACT.Exp)
                    tick(ins, exp_done)
                elif s.kind == "turn":
                    for i, use in enumerate(u):
                        if i % 2 == 0:
                            full(act, use)
                            e, t = (i // 2, i % 2) if s.branch == "b" else (0, i)
                            free(nc.scalar.activation(
                                probT[:, e, 0:s.kb, t * P:(t + 1) * P],
                                bank(use)[:, 0:s.kb * P].rearrange("p (k q) -> p k q", k=s.kb), ACT.Copy), use)
                elif s.kind == "weigh":
                    full(act, u[0])
                    if s.branch == "b":
                        free(nc.scalar.activation(y[:, s.part, wide(s.stream)], bank(u[0])[:, 0:256], ACT.Copy), u[0])
                    else:
                        free(nc.scalar.activation(
                            o_d[:, 2 * s.stream:2 * s.stream + 2, s.part * P:(s.part + 1) * P],
                            bank(u[0])[:, 0:256].rearrange("p (t e) -> p t e", t=2), ACT.Copy), u[0])
                elif s.kind == "d_root":
                    all_moved(act, s.after)
                    for i, t in enumerate(s.toks):
                        act.wait_ge(ms_ready, s.root + i)
                        act.wait_ge(o_clamped, s.n + i + 1)
                        tick(nc.scalar.activation(sq, (tB, tC)[i][:], ACT.Square, scale=1.0 / BIG ** 0.5), sq_ready)
                elif s.kind == "d_turn":
                    full(act, u[0])
                    free(nc.scalar.activation(y[:, :, s.t * P:(s.t + 1) * P],
                                              bank(u[0]).rearrange("p (i q) -> p i q", i=4),
                                              ACT.Copy, scale=sub_g[:, L:L + 1]), u[0])
                elif s.kind == "fourier_in":
                    for t, use in enumerate(u):
                        full(act, use)
                        free(nc.scalar.activation(u_a[:, t, 0:FW], bank(use)[:, 0:FW], ACT.Copy), use)
                elif s.kind == "fourier_seq":
                    full(act, u[0])
                    free(nc.scalar.activation(f_seq[:, 3 * s.stream + s.i], bank(u[0]), ACT.Copy), u[0])
                elif s.kind == "fourier_dim":
                    full(act, u[0])
                    free(nc.scalar.activation(y[:, s.i, 0:W], bank(u[0])[:, 0:W], ACT.Copy), u[0])
                elif s.kind == "merge" and s.branch == "a" and s.j == KD - 1:
                    full(act, u[0])
                    for k in range(KD):
                        act.wait_ge(mixed_ready, KD * L + k + 1)
                        tick(nc.scalar.activation(h_hi[:, k, 0:W], mixed[:, k, 0:W], ACT.Copy), h_hi_ready)
                elif s.kind == "out" and L == 0 and s.j:
                    moved(act, u[0] - 1)
                    tick(nc.scalar.activation(sq_x[:, s.j - 1], xT[:, s.j - 1], ACT.Square), squares)
                elif s.kind == "turn_out":
                    full(act, u[0])
                    tick(nc.scalar.activation(prob[:, 2 * s.t + s.half], bank(u[0]), ACT.Copy), row_out)

        @block.vector
        def _(dve):
            counts, last = {}, []

            def tick(ins, signal):
                counts[id(signal)] = counts.get(id(signal), 0) + 1
                ins.then_inc(signal, 1)
                last[:] = [signal, counts[id(signal)]]

            def free(ins, use):
                ins.then_inc(bank_free[use % BANKS], 1)
                last[:] = [bank_free[use % BANKS], use // BANKS + 1]

            def settle():
                if last:
                    dve.wait_ge(*last)

            def link(ins):
                tick(ins, dve_own)
                settle()

            split = [0]

            def split_lo(upto):
                while split[0] < min(upto, len(plan.tiles)):
                    m = split[0]
                    kt = plan.tiles[m][3]
                    dve.wait_ge(hi_ready, m + 1)
                    tick(nc.vector.tensor_tensor(w_lo[:, m % HL, 0:kt], w_raw[:, m % RAW, 0:kt],
                                            w_hi[:, m % HL, 0:kt].bitcast(F32), ALU.subtract), lo_ready)
                    split[0] += 1

            def h_lo_part(k, count, W):
                dve.wait_ge(h_hi_ready, count)
                tick(nc.vector.tensor_tensor(h_lo[:, k, 0:W], mixed[:, k, 0:W], h_hi[:, k, 0:W].bitcast(F32),
                                        ALU.subtract), h_lo_ready)

            def z_gate(s, use, y_ap):
                W = SEQ * streams(s.layer)
                dve.wait_ge(tanh_ready, s.z + 1)
                ins = nc.vector.scalar_tensor_tensor(tB[:, 0:W], th[:, 0:W], 1.0, bank(use)[:, 0:W], ALU.add, ALU.mult)
                free(ins, use)
                moved(dve, use)
                tick(nc.vector.tensor_tensor(tC[:, 0:W], tB[:, 0:W], y_ap, ALU.mult), gated)
                dve.wait_ge(g_hi_ready, s.z + 1)
                tick(nc.vector.tensor_tensor(g_lo[:, s.i, 0:W], tC[:, 0:W], g_hi[:, s.i, 0:W].bitcast(F32),
                                        ALU.subtract), g_lo_ready)

            def add_square(layer, k):
                dve.wait_ge(squares, KD * layer + k + 1)
                tick(nc.vector.tensor_tensor(sq_x[:, 0], sq_x[:, 0], sq_x[:, k], ALU.add),
                     sq_summed if k == KD - 1 else dve_own)
                settle()

            waiting = []

            def normalise():
                if not waiting:
                    return
                s = waiting.pop()
                nk = s.kb * P
                dve.wait_ge(exp_done, s.g + 1)
                if s.branch == "b":
                    link(nc.vector.tensor_tensor(sums, sums, sink_e, ALU.add))
                link(nc.vector.reciprocal(inv, sums))
                if s.branch == "b":
                    for i in range(4):
                        ins = nc.vector.tensor_scalar(prob[:, i, 0:nk], prob[:, i, 0:nk], inv[:, i:i + 1], None, ALU.mult)
                else:
                    minus_lam = tail[:, 16 + s.layer:17 + s.layer]
                    nc.vector.tensor_scalar(lam_inv[:, 0:2], inv[:, 2:4], minus_lam, None, ALU.mult)
                    for t in range(2):
                        ins = nc.vector.tensor_scalar(prob[:, t, 0:nk], prob[:, t, 0:nk], inv[:, t:t + 1], None, ALU.mult)
                    link(ins)
                    for t in range(2):
                        ins = nc.vector.scalar_tensor_tensor(prob[:, t, 0:nk], prob[:, 2 + t, 0:nk],
                                                             lam_inv[:, t:t + 1], prob[:, t, 0:nk], ALU.mult, ALU.add)
                tick(ins, prob_ready)

            tick(nc.vector.memset(ones[:], 1.0), ones_set)
            for s in steps:
                L, u = s.layer, s.uses
                settle()
                S = streams(L)
                W = SEQ * S
                if s.kind != "weigh":
                    normalise()
                split_lo(s.first_tile + HL)
                if s.kind == "rows":
                    dve.wait_ge(rows_landed, 16 * 19)
                    lam_v = lam_rows.rearrange("p (a b) l e -> p a b l e", b=2)
                    for i in range(2):
                        ins = nc.vector.tensor_tensor(tA[0:1, 128 * i:128 * i + 128].rearrange("p (l e) -> p l e", l=2),
                                                      lam_v[:, i, 0], lam_v[:, i, 1], ALU.mult)
                    link(ins)
                    tick(nc.vector.tensor_reduce(lam_tmp[:, 0:4], tA[0:1, 0:256].rearrange("p (g e) -> p g e", g=4),
                                            AX.X, ALU.add), lam_sums)
                    dve.wait_ge(lam_exp, 1)
                    link(nc.vector.tensor_tensor(lam_tmp[:, 0:2], lam_tmp[:, 6:8], lam_tmp[:, 4:6], ALU.subtract))
                    for layer in range(DEPTH):
                        ins = nc.vector.tensor_scalar(row[:, 528 + layer:529 + layer], lam_tmp[:, layer:layer + 1],
                                                      -lam_init(layer), None, ALU.add)
                    tick(ins, lam_ready)
                    full(dve, u[0])
                    free(nc.vector.tensor_copy(vec[:], bank(u[0])[:, 0:V_ROWS]), u[0])
                    full(dve, u[1])
                    free(nc.vector.tensor_copy(gains[:].rearrange("p l k e -> p (l k e)"), bank(u[1])), u[1])
                    full(dve, u[2])
                    free(nc.vector.tensor_copy(tail[:], bank(u[2])[:, 0:18]), u[2])
                    moved(dve, u[0])
                    for layer in range(DEPTH):
                        tick(nc.vector.tensor_scalar(sub_g[:, layer:layer + 1], vec[:, V_SUBLN + layer:V_SUBLN + layer + 1],
                                                1.0 - lam_init(layer), None, ALU.mult), vec_ready)
                    dve.wait_ge(c_tanh, 1)
                    tick(nc.vector.scalar_tensor_tensor(sil[:].rearrange("p k s -> p s k"),
                                                   c_th[:].rearrange("p (s k) -> p s k", s=2), 1.0,
                                                   vec[:, V_C:V_C + 16].rearrange("p (s k) -> p s k", s=2),
                                                   ALU.add, ALU.mult), sil_ready)
                    settle()
                    link(nc.vector.tensor_copy(sil4[:, :, 0:2], sil[:]))
                    tick(nc.vector.tensor_tensor(sil4[:, :, 2:4], sil[:], sil4[:, :, 0:2].bitcast(F32),
                                                 ALU.subtract), sil_ready)
                elif s.kind == "mod_turn":
                    full(dve, u[0])
                    bias = vec[:, V_BMOD + 24 * L + s.j0:V_BMOD + 24 * L + s.j0 + s.n]
                    sums_v = tA[:, 0:2 * s.n].rearrange("p (j s) -> p j s", s=2)
                    free(nc.vector.tensor_reduce(sums_v, bank(u[0])[:, 0:4 * s.n].rearrange("p (j a s) -> p j s a", a=2, s=2),
                                                 AX.X, ALU.add), u[0])
                    moved(dve, u[0])
                    link(nc.vector.scalar_tensor_tensor(modv[:, s.j0:s.j0 + s.n, :], sums_v, 0.5,
                                                        bias.unsqueeze(2).to_broadcast([P, s.n, 2]),
                                                        ALU.mult, ALU.add))
                    if s.j0 == 0:
                        g = vec[:, V_NORM + KD * L:V_NORM + KD * (L + 1)]
                        tick(nc.vector.scalar_tensor_tensor(amp[:], modv[:, KD:2 * KD, :], 1.0,
                                                       g.unsqueeze(2).to_broadcast([P, KD, 2]),
                                                       ALU.add, ALU.mult), mod_ready)
                    else:
                        link(nc.vector.tensor_scalar(gatev[:], modv[:, 2 * KD:3 * KD, :], 0.25, None, ALU.mult))
                elif s.kind == "norm":
                    if L == 0:
                        dve.wait_ge(const_landed, 16 * 4)
                        moved(dve, 1)
                    for kd in range(4):
                        gain = gains[:, L, kd]
                        nc.vector.tensor_tensor(rope_g[:, kd, 0], rope[:, 0],
                                                gain.unsqueeze(1).to_broadcast([P, 2, HD]), ALU.mult)
                        to = rope_g[:, kd, 1].rearrange("p t (g s e) -> p t g s e", g=2, s=2)
                        sn = rope[:, 1].rearrange("p t (g s e) -> p t g s e", g=2, s=2)
                        gv = gain.rearrange("p (g s e) -> p g s e", g=2, s=2)
                        for h in range(2):
                            ins = nc.vector.tensor_tensor(to[:, :, :, h], sn[:, :, :, h],
                                                          gv[:, :, 1 - h].unsqueeze(1).to_broadcast([P, 2, 2, 16]),
                                                          ALU.mult)
                    link(ins)
                    for k in range(1 if L == 0 else KD - 1, KD):
                        add_square(L, k)
                    full(dve, u[0])
                    r = s.root
                    ins = nc.vector.tensor_scalar(ms[:, r % 2], bank(u[0])[:, 0:4], 1.0 / D, EPS, ALU.mult, ALU.add)
                    tick(ins, ms_ready)
                    dve.wait_ge(rms_ready, r + 1)
                    free(nc.vector.tensor_copy(tB[:, 0:4], bank(u[0])[:, 0:4]), u[0])
                    for t in range(4):
                        ins = nc.vector.tensor_scalar(diag[:, t], ident[:], rms[:, r % 2, t:t + 1], None, ALU.mult)
                    tick(ins, diag_ready)
                    full(dve, u[1])
                    for k in range(KD):
                        ins = nc.vector.tensor_tensor(mixed[:, k], xT[:, k], bank(u[1]), ALU.mult)
                        tick(ins, scaled)
                        if k:
                            h_lo_part(k - 1, 2 * KD * L + k, TOK)
                    h_lo_part(KD - 1, 2 * KD * L + KD, TOK)
                    free(nc.vector.tensor_copy(tB[:, 0:4], bank(u[1])[:, 0:4]), u[1])
                elif s.kind == "tokens" and s.name != "d_v":
                    nh = 2 if s.name == "b_k" else 4
                    n = nh * HD
                    kd = KINDS.index(s.name)
                    for use, t, q, r in ((u[0], s.t, s.qk, s.root),):
                        dve.wait_ge(sq_ready, r - L)
                        link(nc.vector.tensor_reduce(tA[:, 0:nh], sq[:, 0:n].rearrange("p (h e) -> p h e", e=HD),
                                                     AX.X, ALU.add))
                        tick(nc.vector.tensor_scalar(ms[:, r % 2, 0:nh], tA[:, 0:nh], 1.0 / HD, EPS,
                                                ALU.mult, ALU.add), ms_ready)
                        ps = bank(use)[:, 0:n].rearrange("p (h e) -> p h e", e=HD)
                        tb = tB[:, 0:n].rearrange("p (h e) -> p h e", e=HD)
                        if t < 2:
                            nc.vector.tensor_tensor(tb, ps, rope_g[:, kd, 0, t].unsqueeze(1).to_broadcast([P, nh, HD]),
                                                    ALU.mult)
                            p5 = bank(use)[:, 0:n].rearrange("p (h g s e) -> p h g s e", g=2, s=2, e=16)
                            t5 = tC[:, 0:n].rearrange("p (h g s e) -> p h g s e", g=2, s=2, e=16)
                            sn = rope_g[:, kd, 1, t].rearrange("p (g s e) -> p g s e", g=2, s=2)
                            for h in range(2):
                                ins = nc.vector.tensor_tensor(t5[:, :, :, h], p5[:, :, :, 1 - h],
                                                              sn[:, :, h].unsqueeze(1).to_broadcast([P, nh, 2, 16]),
                                                              ALU.mult)
                            free(ins, use)
                            moved(dve, use)
                            link(nc.vector.tensor_tensor(tB[:, 0:n], tB[:, 0:n], tC[:, 0:n], ALU.add))
                        else:
                            free(nc.vector.tensor_tensor(tb, ps, gains[:, L, kd].unsqueeze(1).to_broadcast([P, nh, HD]),
                                                         ALU.mult), use)
                            moved(dve, use)
                        dve.wait_ge(rms_ready, r + 1)
                        if q >= 4:
                            full(dve, turn_of[q - 4])
                        tick(nc.vector.tensor_tensor(qn[:, q % 4, 0:n].rearrange("p (h e) -> p h e", e=HD), tb,
                                                rms[:, r % 2, 0:nh].unsqueeze(2).to_broadcast([P, nh, HD]),
                                                ALU.mult), qn_ready)
                elif s.kind == "conv":
                    full(dve, u[1])
                    cu = conv_u[:, 0:S]
                    if s.i == 0:
                        nc.vector.memset(conv_u[:, :, 0:1], 0.0)
                        nc.vector.memset(conv_u[:, :, 257:258], 0.0)
                    moved(dve, u[0])
                    free(nc.vector.tensor_tensor(cu[:, :, 1:257], conv_x[:, 0:W].rearrange("p (s t) -> p s t", s=S),
                                                 bank(u[1])[:, 0:W].rearrange("p (s t) -> p s t", s=S), ALU.mult), u[1])
                    moved(dve, u[1])
                    ta = tA[:, 0:W].rearrange("p (s t) -> p s t", s=S)
                    tap = [vec[:, V_CONV + 9 * L + 3 * j + s.i:V_CONV + 9 * L + 3 * j + s.i + 1] for j in range(3)]
                    link(nc.vector.tensor_scalar(ta, cu[:, :, 0:256], tap[0], None, ALU.mult))
                    for j in (1, 2):
                        link(nc.vector.scalar_tensor_tensor(ta, cu[:, :, j:j + 256], tap[j], ta, ALU.mult, ALU.add))
                    split_lo(s.first_tile + HL + 1)
                    full(dve, u[2])
                    free(nc.vector.tensor_tensor(tA[:, 0:W], tA[:, 0:W], bank(u[2])[:, 0:W], ALU.mult), u[2])
                    moved(dve, u[2])
                    split_lo(s.first_tile + HL + 3)
                    z_gate(s, u[3], tA[:, 0:W])
                elif s.kind == "silu":
                    all_moved(dve, u[0])
                    z_gate(s, u[0], y[:, s.i, 0:W])
                elif s.kind == "merge":
                    full(dve, u[0])
                    moved(dve, s.gate)
                    gate = gate_t[:, s.n % 2, 0:W]
                    if s.branch == "c":
                        free(nc.vector.scalar_tensor_tensor(mixed[:, s.j, 0:W], gate, 1.0, bank(u[0])[:, 0:W],
                                                            ALU.add, ALU.mult), u[0])
                    else:
                        free(nc.vector.scalar_tensor_tensor(tB[:, 0:W], gate, 1.0, bank(u[0])[:, 0:W],
                                                            ALU.add, ALU.mult), u[0])
                        moved(dve, u[0])
                        ins = nc.vector.tensor_tensor(mixed[:, s.j, 0:W], mixed[:, s.j, 0:W], tB[:, 0:W], ALU.add)
                        tick(ins, mixed_ready if s.branch == "a" else dve_own)
                        if s.branch == "a":
                            if s.j == KD - 1:
                                for k in range(KD):
                                    h_lo_part(k, 2 * KD * L + KD + k + 1, W)
                elif s.kind == "out":
                    full(dve, u[0])
                    for st in range(S):
                        ins = nc.vector.scalar_tensor_tensor(xT[:, s.j, wide(st)], bank(u[0])[:, wide(st)],
                                                             gatev[:, s.j, st:st + 1], xT[:, s.j, wide(st)],
                                                             ALU.mult, ALU.add)
                    free(ins, u[0])
                    if L == 0 and s.j >= 2:
                        settle()
                        add_square(1, s.j - 1)
                elif s.kind == "score":
                    nk = s.kb * P
                    dve.wait_ge(scores_done, s.g + 1)
                    if s.branch == "b" and s.stream == 0:
                        sv = score_ps[:].rearrange("p (e t) k -> p e t k", e=2)
                        for t, c0 in ((0, P), (1, 0)):
                            o = sv[:, :, t, c0:c0 + P]
                            ins = nc.vector.tensor_tensor(o, o, masks[:, t].unsqueeze(1).to_broadcast([P, 2, P]), ALU.add)
                        link(ins)
                    link(nc.vector.tensor_reduce(top, score_ps[:, :, 0:nk], AX.X, ALU.max))
                    if s.branch == "b":
                        c0 = 8 * L + 2 * s.part
                        sink = tail[:, c0:c0 + 2].unsqueeze(2).to_broadcast([P, 2, 2])
                        low_v = low.rearrange("p (e t) -> p e t", e=2)
                        link(nc.vector.scalar_tensor_tensor(low_v, top.rearrange("p (e t) -> p e t", e=2), SCALE, sink,
                                                            ALU.mult, ALU.max))
                        nc.vector.tensor_tensor(sink_d.rearrange("p (e t) -> p e t", e=2), sink, low_v, ALU.subtract)
                        tick(nc.vector.tensor_scalar(negmax, low, -1.0, None, ALU.mult), negmax_ready)
                    else:
                        tick(nc.vector.tensor_scalar(negmax, top, -SCALE, None, ALU.mult), negmax_ready)
                    waiting.append(s)
                elif s.kind == "turn":
                    for i, use in enumerate(u):
                        if i % 2:
                            full(dve, use)
                            e, t = (i // 2, i % 2) if s.branch == "b" else (0, i)
                            free(nc.vector.tensor_copy(
                                probT[:, e, 0:s.kb, t * P:(t + 1) * P],
                                bank(use)[:, 0:s.kb * P].rearrange("p (k q) -> p k q", k=s.kb)), use)
                elif s.kind == "d_root":
                    def clamp(t):
                        tick(nc.vector.tensor_scalar((tB, tC)[t % 2][:], o_d[:, t], BIG, -BIG, ALU.min, ALU.max),
                             o_clamped)

                    all_moved(dve, s.after)
                    clamp(s.toks[0])
                    for i, t in enumerate(s.toks):
                        r = s.root + i
                        dve.wait_ge(sq_ready, r - L)
                        if i + 1 < len(s.toks):
                            clamp(t + 1)
                            settle()
                        link(nc.vector.tensor_reduce(tA[:, 0:4], sq.rearrange("p (h e) -> p h e", e=P),
                                                     AX.X, ALU.add))
                        link(nc.vector.tensor_scalar(tA[:, 4:8], tA[:, 0:4], BIG, BIG / P, ALU.min, ALU.mult))
                        tick(nc.vector.tensor_scalar(ms[:, r % 2], tA[:, 4:8], EPS, None, ALU.add), ms_ready)
                        dve.wait_ge(rms_ready, r + 1)
                        link(nc.vector.scalar_tensor_tensor(tA[:, 8:12], tA[:, 0:4], BIG, rms[:, r % 2],
                                                            ALU.is_lt, ALU.mult))
                        o = o_d[:, t].rearrange("p (h e) -> p h e", e=P)
                        tick(nc.vector.tensor_tensor(o, o, tA[:, 8:12].unsqueeze(2).to_broadcast([P, 4, P]),
                                                     ALU.mult), o_normed)


def constants():
    n = np.arange(SEQ)
    seq = 2 * np.pi * ((n[:, None] * n[None, :]) % SEQ) / SEQ
    cs = np.concatenate([np.cos(seq), np.sin(seq)], axis=1).astype(np.float32)
    d = np.arange(HD)
    dim = 2 * np.pi * ((d[:, None] * d[None, :]) % HD) / HD
    norm = 1.0 / math.sqrt(SEQ * HD)
    dft_dim = np.stack([np.kron(np.eye(2), np.cos(dim) * norm), np.kron(np.eye(2), -np.sin(dim) * norm)], axis=1)
    nf = HD // 4
    freq = np.float32(10000.0) ** (-np.arange(nf, dtype=np.float32) / np.float32(nf))
    ar = (n // GRID_W).astype(np.float32)[:, None] * freq[None, :]
    ac = (n % GRID_W).astype(np.float32)[:, None] * freq[None, :]
    cos = np.concatenate([np.cos(ar), np.cos(ar), np.cos(ac), np.cos(ac)], axis=1)
    sin = np.concatenate([-np.sin(ar), np.sin(ar), -np.sin(ac), np.sin(ac)], axis=1)
    rope = np.stack([cos, sin]).reshape(2, 2, P, HD).transpose(2, 0, 1, 3)
    q = np.arange(P)[:, None]
    k = np.arange(P)[None, :]
    masks = np.stack([np.where(k + P - q <= WINDOW, 0.0, MASKED), np.where(q + P - k <= WINDOW, 0.0, MASKED)], axis=1)
    return {
        "ident": np.eye(P, dtype=np.float32),
        "dft_seq": np.ascontiguousarray(cs.reshape(2, P, 2 * SEQ).transpose(1, 0, 2)),
        "dft_dim": np.ascontiguousarray(dft_dim.astype(np.float32)),
        "rope": np.ascontiguousarray(rope.astype(np.float32)),
        "masks": np.ascontiguousarray(masks.astype(np.float32)),
    }


_INS = ["x", "c", "ctx", "c_ctx", "norm_g", "w_mod", "b_mod", "w_in", "q_norm_b", "k_norm_b", "sink_b",
        "conv_w", "q_norm_d", "k_norm_d", "lam_q1", "lam_k1", "lam_q2", "lam_k2", "subln_d",
        "w_o_a", "w_o_b", "w_o_c", "w_o_d", "w_out"]


def kernel(**inputs):
    import concourse.bacc as bacc
    from concourse.bass_utils import run_bass_kernel_spmd

    nc = bacc.Bacc("TRN2", target_bir_lowering=False, num_devices=1)
    arrays, ins, consts = {}, {}, {}
    for name in _INS:
        v = np.ascontiguousarray(inputs[name])
        arrays[f"in_{name}"] = v
        ins[name] = nc.dram_tensor(f"in_{name}", v.shape, mybir.dt.from_np(v.dtype), kind="ExternalInput").ap()
    for name, v in constants().items():
        arrays[f"const_{name}"] = v
        consts[name] = nc.dram_tensor(f"const_{name}", v.shape, mybir.dt.from_np(v.dtype), kind="ExternalInput").ap()
    out = nc.dram_tensor("out_0", (1, SEQ, D), F32, kind="ExternalOutput").ap()
    hybrid_backbone(nc, ins, consts, out)
    r = run_bass_kernel_spmd(nc, [arrays], core_ids=[0])
    return r.results[0]["out_0"]
```

```python
import math
from contextlib import ExitStack

import numpy as np

import concourse.bass as bass
from concourse import mybir

F32 = mybir.dt.float32
F32R = mybir.dt.float32r
ALU = mybir.AluOpType
ACT = mybir.ActivationFunctionType
AX = mybir.AxisListType

P = 128
D = 1024
KD = D // P
SEQ = 256
CTX = 256
TOK = SEQ + CTX
DEPTH = 2
GRID_W = 64
HD = 64
FW, SW, KV, CW, DW = 384, 512, 128, 384, 512
WINDOW = 128
EPS = 1e-6
SCALE = HD ** -0.5
MASKED = -1e30
BIG = 2.0 ** 64

_NAMES = ("a_x", "b_q", "b_k", "b_v", "c_x", "c_b", "c_c", "d_q", "d_k", "d_v",
          "z_a", "z_b", "z_c", "z_d", "m_g")
_WIDTHS = (FW, SW, KV, KV, CW, CW, CW, DW, DW, DW, FW, SW, CW, DW, 4 * D)
COL = dict(zip(_NAMES, np.cumsum((0,) + _WIDTHS[:-1]).tolist()))

UNSPLIT = 16
RAW = 4
HL = 4
BANKS = 4

V_NORM, V_BMOD, V_CONV, V_SUBLN, V_C, V_ROWS = 0, 16, 64, 82, 84, 100
KINDS = ("b_q", "b_k", "d_q", "d_k")


def lam_init(layer):
    return 0.8 - 0.6 * math.exp(-0.3 * layer)


class Step:

    def __init__(self, kind, layer, *, branch=None, stream=None, part=None, g=None, kb=None, after=None,
                 turned=None, j=None, n=None, used=None, kt=None, gate=None, n_g=None, name=None, w=None,
                 toks=None, qk=None, root=None, t=None, q=None, k=None, j0=None, x_uses=None, i=None,
                 z=None, before=None, weighed=None, half=None):
        self.kind, self.layer = kind, layer
        self.tiles, self.uses, self.first_tile = [], [], 0
        self.branch, self.stream, self.part, self.g, self.kb = branch, stream, part, g, kb
        self.after, self.turned, self.weighed, self.before = after, turned, weighed, before
        self.j, self.n, self.used, self.kt, self.gate, self.n_g = j, n, used, kt, gate, n_g
        self.name, self.w, self.toks, self.qk, self.root = name, w, toks, qk, root
        self.t, self.q, self.k, self.j0, self.x_uses = t, q, k, j0, x_uses
        self.i, self.z, self.half = i, z, half


class Plan:

    def __init__(self):
        self.steps, self.tiles, self.last_use = [], [], []
        self.uses = self.groups = self.qk = self.roots = self.z = self.gates = self.normed = 0

    def add(self, kind, layer, sources=(), uses=1, **kw):
        s = Step(kind, layer, **kw)
        s.uses = list(range(self.uses, self.uses + uses))
        self.uses += uses
        s.first_tile = len(self.tiles)
        for i, src in enumerate(sources):
            s.tiles.append(len(self.tiles))
            self.tiles.append(src)
            self.last_use.append(s.uses[i] if kind == "conv" else s.uses[-1])
        self.steps.append(s)
        return s

    def attention(self, branch, layer, after):
        groups = []
        for stream in range(2 if layer == 0 else 1):
            for part in range(4):
                groups.append(dict(branch=branch, stream=stream, part=part, g=self.groups,
                                   kb=4 if stream == 0 else 2, after=after))
                self.groups += 1
        turns = 4 if branch == "b" else 2
        periods = []
        for i in range(len(groups) + 1):
            micro = []
            if i:
                micro.append(("turn", turns, groups[i - 1]))
            if i < len(groups):
                micro.append(("score", 0, groups[i]))
            if i:
                micro.append(("weigh", 1, groups[i - 1]))
            periods.append(micro)
        return periods


def make_plan():
    p = Plan()
    turn_use = {}

    def w_in(layer, col):
        return ("w_in", layer, col, KD)

    def silu_gate(layer, name, i):
        p.add("silu", layer, [w_in(layer, COL[name] + i * P)], i=i, z=p.z)
        p.z += 1

    conv_before = [None]

    def conv(layer, i):
        s = p.add("conv", layer, [w_in(layer, COL[x] + i * P) for x in ("c_x", "c_c", "c_b", "z_c")],
                  uses=4, i=i, z=p.z, before=conv_before[0] if i else None)
        conv_before[0] = s.uses[1]
        p.z += 1

    def attend(layer, kind, uses, group):
        s = p.add(kind, layer, uses=uses, **group)
        if kind == "turn":
            turn_use[s.g] = s.uses[-1]
        if kind == "score":
            s.turned = turn_use.get(s.g - 1)
        if kind == "weigh":
            s.after = turn_use[s.g] + 1

    def merge_phase(layer, branch, index, periods, mods=()):
        def add_mods(j):
            for at, step in mods:
                if at == j:
                    step()

        n_g = p.z
        merges = []
        for j in range(KD + 1):
            lo, hi = (len(periods) - 1) * j // KD, (len(periods) - 1) * (j + 1) // KD
            if layer:
                lo, hi = (j // 2, j // 2 + 1) if j % 2 == 0 and j < KD else (0, 0)
                if j == KD - 1:
                    lo, hi = KD // 2, KD // 2 + 1
            elif j == KD:
                hi = len(periods)
            held = []
            for period in periods[lo:hi] if periods else []:
                for micro in period:
                    if micro[0] == "weigh" and j < KD:
                        held.append(micro)
                        continue
                    if micro[0] == "weigh" and branch == "d":
                        silu_gate(layer, "z_b", 0)
                    attend(layer, *micro)
            if j == KD:
                break
            even = len(p.tiles) % 2 == 0
            if even:
                add_mods(j)
            s = p.add("gate", layer, [w_in(layer, COL["m_g"] + index * D + j * P)], j=j,
                      n=p.gates, used=merges[-2] if j >= 2 else None)
            p.gates += 1
            for micro in held:
                attend(layer, *micro)
            kt = 3 if branch in "ac" else 4
            if not even:
                add_mods(j)
            m = p.add("merge", layer, [("w_o_" + branch, layer, j * P, kt)], j=j, kt=kt,
                      branch=branch, n=s.n, gate=s.uses[0], n_g=n_g)
            merges.append(m.uses[0])

    waiting = []

    def turn_waiting(layer, left, in_use=None):
        while len(waiting) > left:
            s = p.add("turn_qk", layer, **waiting.pop(0))
            if in_use is not None:
                s.first_tile = in_use

    def tokens(layer, name, w, src, toks):
        first = len(p.tiles)
        for t in toks:
            last = p.uses
            s = p.add("tokens", layer, src if t == toks[0] else [], name=name, w=w, t=t, qk=p.qk, root=p.roots)
            s.tiles, s.first_tile = [first, first + 1], first
            if name != "d_v":
                waiting.append(dict(name=name, w=w, t=t, q=p.qk))
                p.qk += 1
                p.roots += 1
            turn_waiting(layer, 2, first if t != toks[-1] else None)
        p.last_use[first] = p.last_use[first + 1] = last

    def modulation(layer, j0, n):
        def mod(w):
            assert len(p.tiles) % 2 == 0
            s = p.add("mod", layer, [("w_mod", layer, (j0 + 2 * w + i) * P, KD) for i in range(2)], w=w)
            mod_use[0] = s.uses[0]

        def turn():
            p.add("mod_turn", layer, j0=j0, n=n, after=mod_use[0])

        return [lambda w=w: mod(w) for w in range(n // 2)] + [turn]

    mod_use = [0]

    def statistics(layer, between=()):
        p.add("stats", layer, uses=1, root=p.roots, x_uses=x_uses)
        p.roots += 1
        for step in between:
            step()
        p.add("spread", layer, uses=0)

    x_uses = None
    p.add("c_vectors", 0)
    mods = modulation(0, 0, 16)
    for step in mods[0:2]:
        step()
    p.add("vectors", 0)
    for k in range(KD):
        p.add("turn_x", 0, k=k)
        if k % 4 == 3:
            mods[2 + k // 4]()
    mods[4]()
    statistics(0, mods[5:6])
    for step in mods[6:9]:
        step()
    p.steps[-1].first_tile = p.steps[-2].first_tile
    for layer in range(DEPTH):
        both = layer == 0
        if layer:
            statistics(layer)
        p.add("modulate", layer, uses=0)
        conv(layer, 0)
        if both:
            p.add("lambda", 0, uses=0)
        conv(layer, 1)
        if both:
            p.add("rows", 0, uses=2)
        for w in range(2):
            for name in ("d_k", "d_q", "d_v"):
                toks = list(range(4 if both or name != "d_q" else 2))
                c0 = COL[name] + 2 * P * w
                tokens(layer, name, w, [w_in(layer, c0), w_in(layer, c0 + P)], toks)
        turn_waiting(layer, 0)
        after = p.uses
        conv(layer, 2)
        merge_phase(layer, "c", 2, p.attention("d", layer, after))

        def d_root(toks):
            p.add("d_root", layer, uses=0, toks=toks, root=p.roots, n=p.normed, after=p.uses)
            p.roots += len(toks)
            p.normed += len(toks)
            return [dict(t=t, n=p.normed - len(toks) + i) for i, t in enumerate(toks)]

        turns = d_root([0, 1]) + (d_root([2, 3]) if both else [])
        assert len(p.tiles) % HL == 0
        p.add("fourier_in", layer, [w_in(layer, COL["a_x"] + n * P) for n in range(3)], uses=4 if both else 2)
        for t in turns:
            p.add("d_turn", layer, **t)
        silu_gate(layer, "z_d", 0)
        for w in (2, 0, 1):
            toks = list(range(4 if both or w == 2 else 2))
            if w < 2:
                src = [("heads", layer, COL["b_q"] + (2 * w + i) * HD, KD) for i in range(2)]
            else:
                src = [w_in(layer, COL["b_k"]), w_in(layer, COL["b_v"])]
            tokens(layer, "b_q" if w < 2 else "b_k", w, src, toks)
        silu_gate(layer, "z_d", 1)
        turn_waiting(layer, 0)
        after = p.uses
        for i in (2, 3):
            silu_gate(layer, "z_d", i)
        n_z = p.z
        merge_phase(layer, "d", 3, p.attention("b", layer, after))
        weighed = [s for s in p.steps if s.kind == "weigh"][-1].uses[0]
        for i in range(p.z - n_z, 4):
            silu_gate(layer, "z_b", i)
        p.steps[-1].weighed = weighed
        after = p.uses
        merge_phase(layer, "b", 1, [], list(zip((0, 2, 4, 6, 7), modulation(layer, 16, 8))))
        for s in range(2 if both else 1):
            for i in range(3):
                p.add("fourier_seq", layer, stream=s, i=i, after=after)
        after = p.uses
        for i in range(3):
            p.add("fourier_dim", layer, i=i, after=after)
        for i in range(3):
            silu_gate(layer, "z_a", i)
        mods = modulation(1, 0, 16) if both else []
        merge_phase(layer, "a", 0, [], list(zip(range(KD), mods)))
        x_uses = []
        for j in range(KD):
            s = p.add("out", layer, [("w_out", layer, j * P, KD)], j=j)
            x_uses.append(s.uses[0])
            if both and j == 0:
                mods[KD]()
    after = p.uses
    for t in range(2):
        for half in range(2):
            p.add("turn_out", 1, t=t, half=half, after=after)
    return p


def hybrid_backbone(nc, a, c, out):
    plan = make_plan()
    steps = plan.steps
    with ExitStack() as ctx:
        def sb(name, shape, dt=F32):
            return ctx.enter_context(nc.sbuf_tensor(name, shape, dt))

        def sem(name):
            return ctx.enter_context(nc.semaphore(name))

        xT = sb("xT", [P, KD, TOK])
        h_hi = sb("h_hi", [P, KD, TOK], F32R)
        h_lo = sb("h_lo", [P, KD, TOK], F32R)
        mixed = sb("mixed", [P, KD, TOK])
        w_raw = sb("w_raw", [P, RAW, KD, P])
        w_hi = sb("w_hi", [P, HL, KD, P], F32R)
        w_lo = sb("w_lo", [P, HL, KD, P], F32R)
        qkv = sb("qkv", [P, 3, 4, TOK])
        y = sb("y", [P, 4, TOK])
        o_d = sb("o_d", [P, 4, TOK])
        g_hi = sb("g_hi", [P, 4, TOK], F32R)
        g_lo = sb("g_lo", [P, 4, TOK], F32R)
        prob = sb("prob", [P, 4, TOK])
        probT = sb("probT", [P, 2, 4, 256])
        gate_t = sb("gate_t", [P, 2, TOK])
        tA = sb("tA", [P, TOK])
        tB = sb("tB", [P, TOK])
        tC = sb("tC", [P, TOK])
        ident = sb("ident", [P, P])
        ones = sb("ones", [P, P])
        dft_dim = sb("dft_dim", [P, 2, P])
        rope = sb("rope", [P, 2, 2, HD])
        rope_g = sb("rope_g", [P, 4, 2, 2, HD])
        masks = sb("masks", [P, 2, P])
        vec = sb("vec", [P, V_ROWS])
        gains = sb("gains", [P, DEPTH, 4, HD])
        tail = sb("tail", [P, 18])
        c_th = sb("c_th", [P, 16])
        sil = sb("sil", [P, KD, 2])
        sil0 = sb("sil0", [P, KD, 4])
        sil4 = sb("sil4", [P, KD, 4], F32R)
        modv = sb("modv", [P, 24, 2])
        amp = sb("amp", [P, KD, 2])
        gatev = sb("gatev", [P, KD, 2])
        ms = sb("ms", [P, 2, 4])
        rms = sb("rms", [P, 2, 4])
        minus_half = sb("minus_half", [P, 4])
        sm = sb("sm", [P, 32])
        sub_g = sb("sub_g", [P, DEPTH])
        lam_tmp = sb("lam_tmp", [1, 8])
        top, low, negmax, sink_d, sums, sink_e, inv, lam_inv = (sm[:, 4 * i:4 * i + 4] for i in range(8))

        qT, kT, v_tok = qkv[:, 0], qkv[:, 1], qkv[:, 2]
        x_in = qkv[:, 0:2].rearrange("p a b t -> p (a b t)").rearrange("p (t d) -> p t d", d=D)
        h_full = qkv[:, 0:2].rearrange("p a b t -> p (a b) t")
        sq_x = mixed
        vec_rows = gate_t[0:V_C, 1, 0:P]
        c_rows = gate_t[0:16, 1, P:2 * P]
        row = probT[0:1, 1, 0:3].rearrange("p a t -> p (a t)")
        lam_rows = gate_t[0:1, 0].rearrange("p (i l e) -> p i l e", i=4, l=2)
        mod_rows = prob[0:4].rearrange("p a t -> p (a t)")
        diag = tA[:].rearrange("p (t q) -> p t q", t=4)
        conv_x = probT[:, 0, 0:2].rearrange("p a t -> p (a t)")
        conv_u = prob[:, 0:2].rearrange("p a t -> p (a t)")[:, 0:2 * 258].rearrange("p (s t) -> p s t", s=2)
        qn = prob[:, 2:4].rearrange("p a t -> p (a t)").rearrange("p (r n) -> p r n", n=256)
        sq, th = gate_t[:, 0], gate_t[:, 1]
        dft_seq = probT[:, 0].rearrange("p k t -> p (k t)").rearrange("p (a n) -> p a n", a=2)
        u_a = kT[:, 1:4].rearrange("p a t -> p (a t)").rearrange("p (t n) -> p t n", n=FW)
        f_seq = [(qT if n < 4 else v_tok)[:, n % 4] for n in range(6)]

        score_ps = ctx.enter_context(nc.psum_tensor("score_ps", [P, 4, TOK], F32))
        work_ps = ctx.enter_context(nc.psum_tensor("work_ps", [P, BANKS, TOK], F32))

        raw_landed = [sem(f"raw_landed{i}") for i in range(RAW)]
        bank_full = [sem(f"bank_full{i}") for i in range(BANKS)]
        bank_free = [sem(f"bank_free{i}") for i in range(BANKS)]
        sq_summed = sem("sq_summed")
        hi_ready = sem("hi_ready")
        lo_ready = sem("lo_ready")
        x_landed = sem("x_landed")
        const_landed = sem("const_landed")
        dft_landed = sem("dft_landed")
        c_landed = sem("c_landed")
        vectors_landed = sem("vectors_landed")
        rows_landed = sem("rows_landed")
        ones_set = sem("ones_set")
        c_ready = sem("c_ready")
        c_tanh = sem("c_tanh")
        sil_ready = sem("sil_ready")
        lam_sums = sem("lam_sums")
        lam_exp = sem("lam_exp")
        lam_ready = sem("lam_ready")
        squares = sem("squares")
        half_set = sem("half_set")
        ms_ready = sem("ms_ready")
        rms_ready = sem("rms_ready")
        diag_ready = sem("diag_ready")
        rms_spread = sem("rms_spread")
        mod_ready = sem("mod_ready")
        scaled = sem("scaled")
        modulated = sem("modulated")
        h_hi_ready = sem("h_hi_ready")
        h_lo_ready = sem("h_lo_ready")
        sq_ready = sem("sq_ready")
        qn_ready = sem("qn_ready")
        scores_done = sem("scores_done")
        negmax_ready = sem("negmax_ready")
        exp_done = sem("exp_done")
        prob_ready = sem("prob_ready")
        o_clamped = sem("o_clamped")
        o_normed = sem("o_normed")
        tanh_ready = sem("tanh_ready")
        gated = sem("gated")
        g_hi_ready = sem("g_hi_ready")
        g_lo_ready = sem("g_lo_ready")
        mixed_ready = sem("mixed_ready")
        row_out = sem("row_out")
        stored = sem("stored")
        dve_own = sem("dve_own")

        def full(eng, use):
            eng.wait_ge(bank_full[use % BANKS], use // BANKS + 1)

        def moved(eng, use):
            eng.wait_ge(bank_free[use % BANKS], use // BANKS + 1)

        def all_moved(eng, upto):
            for use in range(max(0, upto - BANKS), upto):
                moved(eng, use)

        def bank(use):
            return work_ps[:, use % BANKS]

        def streams(layer):
            return 2 if layer == 0 else 1

        def wide(s):
            return slice(SEQ * s, SEQ * (s + 1))

        def source(src):
            name, layer, col, kt = src
            w = a["w_in" if name == "heads" else name][layer].rearrange("(k p) n -> p k n", p=P)
            if name == "heads":
                return [(w[:, :, col:col + HD], 0, HD), (w[:, :, col + 4 * HD:col + 5 * HD], HD, HD)]
            return [(w[:, :, col:col + P], 0, P)]

        landed_at, per_slot = [], [0] * RAW
        for n, src in enumerate(plan.tiles):
            per_slot[n % RAW] += 16 * len(source(src))
            landed_at.append(per_slot[n % RAW])

        def raw_wait(eng, n):
            eng.wait_ge(raw_landed[n % RAW], landed_at[n])

        dft_before = {s.tiles[-1] + 1: s.weighed for s in steps if s.weighed is not None}
        turn_of = {s.q: s.uses[0] for s in steps if s.kind == "turn_qk"}

        vector_loads = [(c_rows[0:8], a["c"].rearrange("b (r p) -> (b r) p", p=P)),
                        (c_rows[8:16], a["c_ctx"].rearrange("(r p) -> r p", p=P)),
                        (ident[:], c["ident"]),
                        (vec_rows[V_NORM:V_NORM + 16], a["norm_g"].rearrange("l (r p) -> (l r) p", p=P)),
                        (vec_rows[V_BMOD:V_BMOD + 48], a["b_mod"].rearrange("l (r p) -> (l r) p", p=P)),
                        (vec_rows[V_CONV:V_CONV + 18], a["conv_w"].rearrange("l k (r p) -> (l k r) p", p=P)),
                        (vec_rows[V_SUBLN:V_SUBLN + 2], a["subln_d"])]

        block = ctx.enter_context(nc.Block())

        @block.sync
        def _(sp):
            sp.dma_start(*vector_loads[2]).then_inc(c_landed, 16)
            for n, src in enumerate(plan.tiles):
                if n == RAW:
                    for ap, src_rows in vector_loads[3:]:
                        sp.dma_start(ap, src_rows).then_inc(vectors_landed, 16)
                    for t in range(4):
                        x_src = a["x"][0] if t < 2 else a["ctx"][0]
                        sp.dma_start(x_in[:, t], x_src[(t % 2) * P:(t % 2 + 1) * P, :]).then_inc(x_landed, 16)
                if n >= RAW + UNSPLIT:
                    sp.wait_ge(lo_ready, n - RAW + 1 - UNSPLIT)
                elif n >= RAW:
                    full(sp, plan.last_use[n - RAW])
                if n in dft_before:
                    full(sp, dft_before[n])
                    sp.dma_start(dft_seq, c["dft_seq"]).then_inc(dft_landed, 16)
                for ap, c0, w in source(src):
                    sp.dma_start(w_raw[:, n % RAW, 0:src[3], c0:c0 + w], ap).then_inc(raw_landed[n % RAW], 16)
            for i in range(4):
                sp.wait_ge(row_out, i + 1)
                t, half = i // 2, i % 2
                sp.dma_start(out[0, t * P:(t + 1) * P, half * 512:(half + 1) * 512], prob[:, i]).then_inc(stored, 16)
            sp.wait_ge(stored, 64)

        @block.gpsimd
        def _(pool):
            nc.gpsimd.memset(minus_half[:], -0.5).then_inc(half_set, 1)
            loads = [(row[:, 512:528], a["sink_b"].rearrange("(o l) h -> o (l h)", o=1))]
            for i, name in enumerate(("q_norm_b", "k_norm_b", "q_norm_d", "k_norm_d")):
                for L in range(DEPTH):
                    c0 = (L * 4 + i) * HD
                    loads.append((row[:, c0:c0 + HD], a[name][L:L + 1, :]))
            for i, name in enumerate(("lam_q1", "lam_k1", "lam_q2", "lam_k2")):
                loads.append((lam_rows[:, i], a[name].rearrange("(o l) e -> o l e", o=1)))
            for ap, src in loads:
                pool.dma_start(ap, src).then_inc(rows_landed, 16)
            for ap, name in ((rope, "rope"), (masks, "masks"), (dft_dim, "dft_dim")):
                pool.dma_start(ap[:], c[name]).then_inc(const_landed, 16)
            pool.wait_ge(half_set, 1)
            for s in steps:
                if s.kind == "modulate":
                    pool.wait_ge(mod_ready, s.layer + 1)
                    for k in range(KD):
                        pool.wait_ge(scaled, KD * s.layer + k + 1)
                        for st in range(2):
                            ins = nc.gpsimd.tensor_scalar(h_full[:, k, wide(st)], mixed[:, k, wide(st)],
                                                          amp[:, k, st:st + 1], modv[:, k, st:st + 1],
                                                          ALU.mult, ALU.add)
                        ins.then_inc(modulated, 1)
                if s.kind not in ("stats", "tokens", "d_root") or s.name == "d_v":
                    continue
                for i in range(len(s.toks) if s.kind == "d_root" else 1):
                    r = s.root + i
                    n = 2 if s.kind == "tokens" and s.name == "b_k" else 4
                    pool.wait_ge(ms_ready, r + 1)
                    nc.gpsimd.tensor_tensor(rms[:, r % 2, 0:n], ms[:, r % 2, 0:n], minus_half[:, 0:n],
                                            ALU.pow).then_inc(rms_ready, 1)

        @block.tensor
        def _(pe):
            def claim(use):
                if use >= BANKS:
                    moved(pe, use - BANKS)

            def split_wait(m):
                pe.wait_ge(lo_ready, m + 1 - UNSPLIT)

            def done(ins, use):
                ins.then_inc(bank_full[use % BANKS], 1)

            def project(use, out_ap, tiles, hi, lo, cols, kt, weights_move=False, h_wait=None):
                claim(use)
                for k in range(kt):
                    if h_wait is not None:
                        pe.wait_ge(h_lo_ready, h_wait + k + 1)
                    for i, (wp, hp) in enumerate(((w_hi, hi), (w_hi, lo), (w_lo, hi))):
                        m = tiles[0] % HL
                        h = hp[:, k, cols]
                        if weights_move:
                            lhs, rhs = h, wp[:, m:m + len(tiles), k, :]
                        else:
                            lhs, rhs = wp[:, m, k, :], h
                        last = nc.tensor.matmul(out_ap, lhs, rhs, start=(k == 0 and i == 0),
                                                stop=(k == kt - 1 and i == 2))
                done(last, use)

            for s in steps:
                L, u = s.layer, s.uses
                W = SEQ * streams(L)
                if s.tiles and s.kind != "conv" and s.tiles[0] >= UNSPLIT:
                    split_wait(s.tiles[-1])
                if s.kind == "c_vectors":
                    pe.wait_ge(c_landed, 16 * 3)
                    done(nc.tensor.transpose(bank(u[0])[:, 0:16], c_rows, ident[0:16, 0:16]), u[0])
                elif s.kind == "vectors":
                    claim(u[0])
                    pe.wait_ge(vectors_landed, 16 * 4)
                    done(nc.tensor.transpose(bank(u[0])[:, 0:V_C], vec_rows, ident[0:V_C, 0:V_C]), u[0])
                elif s.kind == "rows":
                    pe.wait_ge(rows_landed, 16 * 13)
                    pe.wait_ge(ones_set, 1)
                    claim(u[0])
                    done(nc.tensor.matmul(bank(u[0]), ones[0:1, :], row[:, 0:512], start=True, stop=True), u[0])
                    claim(u[1])
                    pe.wait_ge(lam_ready, 1)
                    done(nc.tensor.matmul(bank(u[1])[:, 0:18], ones[0:1, :], row[:, 512:530],
                                          start=True, stop=True), u[1])
                elif s.kind == "turn_x":
                    if s.k == 0:
                        pe.wait_ge(x_landed, 16 * 4)
                    claim(u[0])
                    for t in range(4):
                        last = nc.tensor.transpose(bank(u[0])[:, t * P:(t + 1) * P],
                                                   x_in[:, t, s.k * P:(s.k + 1) * P], ident[:])
                    done(last, u[0])
                elif s.kind == "mod":
                    pe.wait_ge(sil_ready, 2)
                    claim(u[0])
                    m = s.tiles[0] % HL
                    if s.tiles[0] < UNSPLIT:
                        for n in s.tiles:
                            raw_wait(pe, n)
                        passes = ((sil0, w_raw),)
                    else:
                        passes = ((sil4, w_hi), (sil4, w_lo))
                    for k in range(KD):
                        for sil_c, w in passes:
                            last = nc.tensor.matmul(bank(u[0])[0:4, 0:256], sil_c[:, k, :], w[:, m:m + 2, k, :],
                                                    start=(k == 0 and w is passes[0][1]),
                                                    stop=(k == KD - 1 and w is passes[-1][1]))
                    done(last, u[0])
                elif s.kind == "mod_turn":
                    moved(pe, s.after)
                    claim(u[0])
                    for i in range(s.n):
                        last = nc.tensor.transpose(bank(u[0])[:, 4 * i:4 * i + 4], mod_rows[:, i * P:(i + 1) * P],
                                                   ident[0:4, 0:4])
                    done(last, u[0])
                elif s.kind == "stats":
                    pe.wait_ge(ones_set, 1)
                    pe.wait_ge(sq_summed, L + 1)
                    claim(u[0])
                    for t in range(4):
                        last = nc.tensor.matmul(bank(u[0])[:, t:t + 1], sq_x[:, 0, t * P:(t + 1) * P],
                                                ones[:, 0:1], start=True, stop=True)
                    done(last, u[0])
                elif s.kind == "spread":
                    for t in range(4):
                        pe.wait_ge(diag_ready, 4 * L + t + 1)
                        last = nc.tensor.matmul(score_ps[:, 0, t * P:(t + 1) * P], ones[:], diag[:, t],
                                                start=True, stop=True)
                    last.then_inc(rms_spread, 1)
                elif s.kind in ("tokens", "fourier_in"):
                    n = P * len(s.tiles)
                    for t, use in enumerate(u, s.t or 0):
                        project(use, bank(use)[:, 0:n], s.tiles, h_hi, h_lo, slice(t * P, (t + 1) * P),
                                KD, True)
                elif s.kind == "turn_qk":
                    claim(u[0])
                    pe.wait_ge(qn_ready, s.q + 1)
                    for i in range(1 if s.name == "b_k" else 2):
                        last = nc.tensor.transpose(bank(u[0])[:, i * P:(i + 1) * P],
                                                   qn[:, s.q % 4, i * P:(i + 1) * P], ident[:])
                    done(last, u[0])
                elif s.kind == "conv" and s.i == 0:
                    beside = [(k, n) for k in range(KD - 2) for n in range(4)]
                    rest = [(k, n) for n in range(4) for k in range(KD - 2, KD)]
                    for k, n in beside + rest:
                        m, use = s.tiles[n], u[n]
                        if k == 0:
                            split_wait(m)
                            claim(use)
                        if n == 0:
                            pe.wait_ge(h_lo_ready, 2 * KD * L + k + 1)
                        for wp, hp in ((w_hi, h_hi), (w_hi, h_lo), (w_lo, h_hi)):
                            last = nc.tensor.matmul(bank(use)[:, 0:W], wp[:, m % HL, k, :], hp[:, k, 0:W],
                                                    start=(k == 0 and hp is h_hi and wp is w_hi),
                                                    stop=(k == KD - 1 and wp is w_lo))
                        if k == KD - 1:
                            done(last, use)
                elif s.kind in ("silu", "conv", "gate"):
                    for m, use in zip(s.tiles, u):
                        if s.kind == "conv":
                            split_wait(m)
                        project(use, bank(use)[:, 0:W], [m], h_hi, h_lo, slice(0, W), KD)
                elif s.kind == "merge":
                    pe.wait_ge(g_lo_ready, s.n_g)
                    project(u[0], bank(u[0])[:, 0:W], s.tiles, g_hi, g_lo, slice(0, W), s.kt)
                elif s.kind == "out":
                    project(u[0], bank(u[0])[:, 0:W], s.tiles, h_hi, h_lo, slice(0, W), KD,
                            h_wait=2 * KD * L + KD if s.j == 0 else None)
                elif s.kind == "score":
                    if s.g:
                        pe.wait_ge(exp_done, s.g)
                    all_moved(pe, s.after)
                    k0, k1 = (0, TOK) if s.stream == 0 else (SEQ, TOK)
                    for i in range(4):
                        e, t = i // 2, i % 2
                        if s.branch == "d":
                            r, q, k = e, qT[:, s.part], kT[:, s.part]
                        else:
                            head = 2 * s.part + e
                            r, q, k = head // 4, qT[:, head % 4], kT[:, 0]
                        q0 = s.stream * SEQ + t * P
                        last = nc.tensor.matmul(score_ps[:, i, 0:k1 - k0], q[r * HD:(r + 1) * HD, q0:q0 + P],
                                                k[r * HD:(r + 1) * HD, k0:k1], start=True, stop=True)
                    last.then_inc(scores_done, 1)
                elif s.kind == "turn":
                    pe.wait_ge(prob_ready, s.g + 1)
                    for i, use in enumerate(u):
                        claim(use)
                        for kb in range(s.kb):
                            last = nc.tensor.transpose(bank(use)[:, kb * P:(kb + 1) * P],
                                                       prob[:, i, kb * P:(kb + 1) * P], ident[:])
                        done(last, use)
                elif s.kind == "weigh":
                    all_moved(pe, s.after)
                    claim(u[0])
                    tb = 0 if s.stream == 0 else 2
                    if s.branch == "b":
                        kv = s.part // 2
                        for e in range(2):
                            for kb in range(s.kb):
                                last = nc.tensor.matmul(
                                    bank(u[0])[e * HD:(e + 1) * HD, 0:256],
                                    v_tok[:, tb + kb, kv * HD:(kv + 1) * HD], probT[:, e, kb, :],
                                    start=(kb == 0), stop=(kb == s.kb - 1))
                    else:
                        for t in range(2):
                            for kb in range(s.kb):
                                last = nc.tensor.matmul(
                                    bank(u[0])[:, t * P:(t + 1) * P], probT[:, 0, kb, t * P:(t + 1) * P],
                                    v_tok[:, tb + kb, s.part * P:(s.part + 1) * P],
                                    start=(kb == 0), stop=(kb == s.kb - 1))
                    done(last, u[0])
                elif s.kind == "d_turn":
                    claim(u[0])
                    pe.wait_ge(o_normed, s.n + 1)
                    for i in range(4):
                        last = nc.tensor.transpose(bank(u[0])[:, i * P:(i + 1) * P],
                                                   o_d[:, s.t, i * P:(i + 1) * P], ident[:])
                    done(last, u[0])
                elif s.kind == "fourier_seq":
                    all_moved(pe, s.after)
                    pe.wait_ge(dft_landed, 16 * (L + 1))
                    pe.wait_ge(const_landed, 16 * 3)
                    claim(u[0])
                    for t in range(2):
                        last = nc.tensor.matmul(bank(u[0]), u_a[:, 2 * s.stream + t, s.i * P:(s.i + 1) * P],
                                                dft_seq[:, t, :], start=(t == 0), stop=(t == 1))
                    done(last, u[0])
                elif s.kind == "fourier_dim":
                    all_moved(pe, s.after)
                    claim(u[0])
                    for st in range(streams(L)):
                        for part in range(2):
                            last = nc.tensor.matmul(bank(u[0])[:, wide(st)], dft_dim[:, part],
                                                    f_seq[3 * st + s.i][:, part * SEQ:(part + 1) * SEQ],
                                                    start=(part == 0), stop=(part == 1))
                    done(last, u[0])
                elif s.kind == "turn_out":
                    all_moved(pe, s.after)
                    claim(u[0])
                    for i in range(4):
                        last = nc.tensor.transpose(bank(u[0])[:, i * P:(i + 1) * P],
                                                   xT[:, 4 * s.half + i, s.t * P:(s.t + 1) * P], ident[:])
                    done(last, u[0])

        @block.scalar
        def _(act):
            counts, last = {}, []

            def tick(ins, signal):
                counts[id(signal)] = counts.get(id(signal), 0) + 1
                ins.then_inc(signal, 1)
                last[:] = [signal, counts[id(signal)]]

            def free(ins, use):
                ins.then_inc(bank_free[use % BANKS], 1)
                last[:] = [bank_free[use % BANKS], use // BANKS + 1]

            def settle():
                if last:
                    act.wait_ge(*last)

            split = [UNSPLIT]

            def split_hi(upto):
                while split[0] < min(upto, len(plan.tiles)):
                    m = split[0]
                    kt = plan.tiles[m][3]
                    raw_wait(act, m)
                    if m >= HL + UNSPLIT:
                        full(act, plan.last_use[m - HL])
                    tick(nc.scalar.activation(w_hi[:, m % HL, 0:kt], w_raw[:, m % RAW, 0:kt], ACT.Copy), hi_ready)
                    split[0] += 1

            for ap, src in vector_loads[0:2]:
                act.dma_start(ap, src).then_inc(c_landed, 16)

            def z_gate(s, use):
                W = SEQ * streams(s.layer)
                all_moved(act, s.uses[0])
                full(act, use)
                tick(nc.scalar.activation(th[:, 0:W], bank(use)[:, 0:W], ACT.Tanh, scale=0.5), tanh_ready)
                act.wait_ge(gated, s.z + 1)
                tick(nc.scalar.activation(g_hi[:, s.i, 0:W], tC[:, 0:W], ACT.Copy), g_hi_ready)

            for s in steps:
                L, u = s.layer, s.uses
                settle()
                W = SEQ * streams(L)
                evac_first = (s.kind == "turn" or s.kind == "mod" and s.tiles[0] < UNSPLIT
                              or s.kind == "merge" and s.branch == "a" and s.j == KD - 1)
                if not evac_first:
                    split_hi(s.first_tile + HL)
                if s.kind == "lambda":
                    act.wait_ge(lam_sums, 1)
                    tick(nc.scalar.activation(lam_tmp[:, 4:8], lam_tmp[:, 0:4], ACT.Exp), lam_exp)
                elif s.kind == "c_vectors":
                    act.wait_ge(c_ready, 1)
                    tick(nc.scalar.activation(c_th[:], vec[:, V_C:V_C + 16], ACT.Tanh, scale=0.5), c_tanh)
                elif s.kind == "mod":
                    full(act, u[0])
                    free(nc.scalar.activation(mod_rows[:, 256 * s.w:256 * (s.w + 1)], bank(u[0])[0:4, 0:256],
                                              ACT.Copy), u[0])
                elif s.kind == "turn_x":
                    full(act, u[0])
                    free(nc.scalar.activation(xT[:, s.k], bank(u[0]), ACT.Copy), u[0])
                    moved(act, u[0])
                    tick(nc.scalar.activation(sq_x[:, s.k], xT[:, s.k], ACT.Square), squares)
                elif s.kind == "stats" and L:
                    moved(act, s.x_uses[KD - 1])
                    tick(nc.scalar.activation(sq_x[:, KD - 1], xT[:, KD - 1], ACT.Square), squares)
                elif s.kind == "modulate":
                    act.wait_ge(mod_ready, L + 1)
                    for k in range(KD):
                        act.wait_ge(scaled, KD * L + k + 1)
                        for st in range(2):
                            ins = nc.scalar.activation(h_hi[:, k, wide(st)], mixed[:, k, wide(st)], ACT.Identity,
                                                       scale=amp[:, k, st:st + 1], bias=modv[:, k, st:st + 1])
                        tick(ins, h_hi_ready)
                elif s.kind == "tokens":
                    for i, (use, t) in enumerate(((u[0], s.t),)):
                        full(act, use)
                        if s.name == "d_v":
                            free(nc.scalar.activation(v_tok[:, t, s.w * 256:(s.w + 1) * 256],
                                                      bank(use)[:, 0:256], ACT.Copy), use)
                            continue
                        if s.name == "b_k":
                            nc.scalar.activation(v_tok[:, t, 0:P], bank(use)[:, P:2 * P], ACT.Copy)
                        n = P if s.name == "b_k" else 256
                        act.wait_ge(ms_ready, s.root + i)
                        tick(nc.scalar.activation(sq[:, 0:n], bank(use)[:, 0:n], ACT.Square), sq_ready)
                elif s.kind == "turn_qk":
                    full(act, u[0])
                    tok = slice(s.t * P, (s.t + 1) * P)
                    if s.name == "b_k":
                        free(nc.scalar.activation(kT[:, 0, tok], bank(u[0])[:, 0:P], ACT.Copy), u[0])
                    else:
                        to = (kT if s.name == "d_k" else qT)[:, 2 * s.w:2 * s.w + 2, tok]
                        free(nc.scalar.activation(to, bank(u[0])[:, 0:256].rearrange("p (a t) -> p a t", a=2),
                                                  ACT.Copy), u[0])
                elif s.kind == "conv":
                    full(act, u[0])
                    split_hi(s.first_tile + HL + 1)
                    if s.before is not None:
                        moved(act, s.before)
                    free(nc.scalar.activation(conv_x[:, 0:W], bank(u[0])[:, 0:W], ACT.Copy), u[0])
                    for i in (2, 3):
                        split_hi(s.first_tile + HL + i)
                    z_gate(s, u[3])
                elif s.kind == "silu":
                    z_gate(s, u[0])
                elif s.kind == "gate":
                    full(act, u[0])
                    if s.used is not None:
                        moved(act, s.used)
                    free(nc.scalar.activation(gate_t[:, s.n % 2, 0:W], bank(u[0])[:, 0:W], ACT.Tanh, scale=0.5), u[0])
                elif s.kind == "score":
                    nk = s.kb * P
                    act.wait_ge(negmax_ready, s.g + 1)
                    if s.turned is not None:
                        full(act, s.turned)
                    for i in range(4):
                        ins = nc.scalar.activation(prob[:, i, 0:nk], score_ps[:, i, 0:nk], ACT.Exp, scale=SCALE,
                                                   bias=negmax[:, i:i + 1], accum_out=sums[:, i:i + 1])
                    if s.branch == "b":
                        ins = nc.scalar.activation(sink_e, sink_d, ACT.Exp)
                    tick(ins, exp_done)
                elif s.kind == "turn":
                    for i, use in enumerate(u):
                        if i % 2 == 0:
                            full(act, use)
                            e, t = (i // 2, i % 2) if s.branch == "b" else (0, i)
                            free(nc.scalar.activation(
                                probT[:, e, 0:s.kb, t * P:(t + 1) * P],
                                bank(use)[:, 0:s.kb * P].rearrange("p (k q) -> p k q", k=s.kb), ACT.Copy), use)
                elif s.kind == "weigh":
                    full(act, u[0])
                    if s.branch == "b":
                        free(nc.scalar.activation(y[:, s.part, wide(s.stream)], bank(u[0])[:, 0:256], ACT.Copy), u[0])
                    else:
                        free(nc.scalar.activation(
                            o_d[:, 2 * s.stream:2 * s.stream + 2, s.part * P:(s.part + 1) * P],
                            bank(u[0])[:, 0:256].rearrange("p (t e) -> p t e", t=2), ACT.Copy), u[0])
                elif s.kind == "d_root":
                    all_moved(act, s.after)
                    for i, t in enumerate(s.toks):
                        act.wait_ge(ms_ready, s.root + i)
                        act.wait_ge(o_clamped, s.n + i + 1)
                        tick(nc.scalar.activation(sq, (tB, tC)[i][:], ACT.Square, scale=1.0 / BIG ** 0.5), sq_ready)
                elif s.kind == "d_turn":
                    full(act, u[0])
                    free(nc.scalar.activation(y[:, :, s.t * P:(s.t + 1) * P],
                                              bank(u[0]).rearrange("p (i q) -> p i q", i=4),
                                              ACT.Copy, scale=sub_g[:, L:L + 1]), u[0])
                elif s.kind == "fourier_in":
                    for t, use in enumerate(u):
                        full(act, use)
                        free(nc.scalar.activation(u_a[:, t, 0:FW], bank(use)[:, 0:FW], ACT.Copy), use)
                elif s.kind == "fourier_seq":
                    full(act, u[0])
                    free(nc.scalar.activation(f_seq[3 * s.stream + s.i], bank(u[0]), ACT.Copy), u[0])
                elif s.kind == "fourier_dim":
                    full(act, u[0])
                    free(nc.scalar.activation(y[:, s.i, 0:W], bank(u[0])[:, 0:W], ACT.Copy), u[0])
                elif s.kind == "merge" and s.branch == "a" and s.j == KD - 1:
                    full(act, s.gate)
                    for k in range(KD):
                        act.wait_ge(mixed_ready, KD * L + k + 1)
                        tick(nc.scalar.activation(h_hi[:, k, 0:W], mixed[:, k, 0:W], ACT.Copy), h_hi_ready)
                elif s.kind == "out" and L == 0 and s.j:
                    moved(act, u[0] - 1)
                    tick(nc.scalar.activation(sq_x[:, s.j - 1], xT[:, s.j - 1], ACT.Square), squares)
                elif s.kind == "turn_out":
                    full(act, u[0])
                    tick(nc.scalar.activation(prob[:, 2 * s.t + s.half], bank(u[0]), ACT.Copy), row_out)
                if evac_first:
                    split_hi(s.first_tile + HL)

        @block.vector
        def _(dve):
            counts, last = {}, []

            def tick(ins, signal):
                counts[id(signal)] = counts.get(id(signal), 0) + 1
                ins.then_inc(signal, 1)
                last[:] = [signal, counts[id(signal)]]

            def free(ins, use):
                ins.then_inc(bank_free[use % BANKS], 1)
                last[:] = [bank_free[use % BANKS], use // BANKS + 1]

            def settle():
                if last:
                    dve.wait_ge(*last)

            def link(ins):
                tick(ins, dve_own)
                settle()

            split = [UNSPLIT]

            def split_lo(upto):
                while split[0] < min(upto, len(plan.tiles)):
                    m = split[0]
                    kt = plan.tiles[m][3]
                    dve.wait_ge(hi_ready, m + 1 - UNSPLIT)
                    tick(nc.vector.tensor_tensor(w_lo[:, m % HL, 0:kt], w_raw[:, m % RAW, 0:kt],
                                            w_hi[:, m % HL, 0:kt].bitcast(F32), ALU.subtract), lo_ready)
                    split[0] += 1

            def lo_part(whole, hi, lo, count):
                dve.wait_ge(h_hi_ready, count)
                tick(nc.vector.tensor_tensor(lo, whole, hi.bitcast(F32), ALU.subtract), h_lo_ready)

            EARLY = 3

            def merged_lo_part(L, k, W):
                lo_part(mixed[:, k, 0:W], h_hi[:, k, 0:W], h_lo[:, k, 0:W], 2 * KD * L + KD + k + 1)

            def h_lo_part(L, k):
                dve.wait_ge(modulated, KD * L + k + 1)
                lo_part(h_full[:, k], h_hi[:, k], h_lo[:, k], 2 * KD * L + k + 1)

            def z_gate(s, use, y_ap):
                W = SEQ * streams(s.layer)
                dve.wait_ge(tanh_ready, s.z + 1)
                ins = nc.vector.scalar_tensor_tensor(tB[:, 0:W], th[:, 0:W], 1.0, bank(use)[:, 0:W], ALU.add, ALU.mult)
                free(ins, use)
                moved(dve, use)
                tick(nc.vector.tensor_tensor(tC[:, 0:W], tB[:, 0:W], y_ap, ALU.mult), gated)
                dve.wait_ge(g_hi_ready, s.z + 1)
                tick(nc.vector.tensor_tensor(g_lo[:, s.i, 0:W], tC[:, 0:W], g_hi[:, s.i, 0:W].bitcast(F32),
                                        ALU.subtract), g_lo_ready)

            def rotation_tables(L):
                for kd in range(4):
                    gain = gains[:, L, kd]
                    nc.vector.tensor_tensor(rope_g[:, kd, 0], rope[:, 0],
                                            gain.unsqueeze(1).to_broadcast([P, 2, HD]), ALU.mult)
                    to = rope_g[:, kd, 1].rearrange("p t (g s e) -> p t g s e", g=2, s=2)
                    sn = rope[:, 1].rearrange("p t (g s e) -> p t g s e", g=2, s=2)
                    gv = gain.rearrange("p (g s e) -> p g s e", g=2, s=2)
                    for h in range(2):
                        ins = nc.vector.tensor_tensor(to[:, :, :, h], sn[:, :, :, h],
                                                      gv[:, :, 1 - h].unsqueeze(1).to_broadcast([P, 2, 2, 16]),
                                                      ALU.mult)
                link(ins)

            def add_square(layer, k):
                dve.wait_ge(squares, KD * layer + k + 1)
                tick(nc.vector.tensor_tensor(sq_x[:, 0], sq_x[:, 0], sq_x[:, k], ALU.add),
                     sq_summed if k == KD - 1 else dve_own)
                settle()

            waiting = []

            def normalise():
                if not waiting:
                    return
                s = waiting.pop()
                nk = s.kb * P
                dve.wait_ge(exp_done, s.g + 1)
                if s.branch == "b":
                    link(nc.vector.tensor_tensor(sums, sums, sink_e, ALU.add))
                link(nc.vector.reciprocal(inv, sums))
                if s.branch == "b":
                    for i in range(4):
                        ins = nc.vector.tensor_scalar(prob[:, i, 0:nk], prob[:, i, 0:nk], inv[:, i:i + 1], None, ALU.mult)
                else:
                    minus_lam = tail[:, 16 + s.layer:17 + s.layer]
                    nc.vector.tensor_scalar(lam_inv[:, 0:2], inv[:, 2:4], minus_lam, None, ALU.mult)
                    for t in range(2):
                        ins = nc.vector.tensor_scalar(prob[:, t, 0:nk], prob[:, t, 0:nk], inv[:, t:t + 1], None, ALU.mult)
                    link(ins)
                    for t in range(2):
                        ins = nc.vector.scalar_tensor_tensor(prob[:, t, 0:nk], prob[:, 2 + t, 0:nk],
                                                             lam_inv[:, t:t + 1], prob[:, t, 0:nk], ALU.mult, ALU.add)
                tick(ins, prob_ready)

            nc.vector.memset(sil0[:], 0.0)
            tick(nc.vector.memset(ones[:], 1.0), ones_set)
            for s in steps:
                L, u = s.layer, s.uses
                settle()
                S = streams(L)
                W = SEQ * S
                if s.kind != "weigh":
                    normalise()
                evac_first = (s.kind in ("turn", "stats") or s.kind == "mod_turn" and s.n == 16
                              or s.kind == "merge" and (s.branch in "cd" or s.branch == "a" and s.j == KD - 1))
                if not evac_first:
                    split_lo(s.first_tile + HL)
                if s.kind == "lambda":
                    dve.wait_ge(rows_landed, 16 * 13)
                    lam_v = lam_rows.rearrange("p (a b) l e -> p a b l e", b=2)
                    for i in range(2):
                        ins = nc.vector.tensor_tensor(tA[0:1, 128 * i:128 * i + 128].rearrange("p (l e) -> p l e", l=2),
                                                      lam_v[:, i, 0], lam_v[:, i, 1], ALU.mult)
                    link(ins)
                    tick(nc.vector.tensor_reduce(lam_tmp[:, 0:4], tA[0:1, 0:256].rearrange("p (g e) -> p g e", g=4),
                                            AX.X, ALU.add), lam_sums)
                    dve.wait_ge(lam_exp, 1)
                    link(nc.vector.tensor_tensor(lam_tmp[:, 0:2], lam_tmp[:, 6:8], lam_tmp[:, 4:6], ALU.subtract))
                    for layer in range(DEPTH):
                        ins = nc.vector.tensor_scalar(row[:, 528 + layer:529 + layer], lam_tmp[:, layer:layer + 1],
                                                      -lam_init(layer), None, ALU.add)
                    tick(ins, lam_ready)
                elif s.kind == "rows":
                    full(dve, u[0])
                    free(nc.vector.tensor_copy(gains[:].rearrange("p l k e -> p (l k e)"), bank(u[0])), u[0])
                    full(dve, u[1])
                    free(nc.vector.tensor_copy(tail[:], bank(u[1])[:, 0:18]), u[1])
                    settle()
                    dve.wait_ge(const_landed, 16 * 3)
                    rotation_tables(0)
                elif s.kind == "vectors":
                    full(dve, u[0])
                    free(nc.vector.tensor_copy(vec[:, 0:V_C], bank(u[0])[:, 0:V_C]), u[0])
                    moved(dve, u[0])
                    for layer in range(DEPTH):
                        tick(nc.vector.tensor_scalar(sub_g[:, layer:layer + 1], vec[:, V_SUBLN + layer:V_SUBLN + layer + 1],
                                                1.0 - lam_init(layer), None, ALU.mult), dve_own)
                elif s.kind == "c_vectors":
                    full(dve, u[0])
                    tick(nc.vector.tensor_copy(vec[:, V_C:V_ROWS], bank(u[0])[:, 0:16]), c_ready)
                    settle()
                    free(nc.vector.tensor_copy(tA[:, 0:4], bank(u[0])[:, 0:4]), u[0])
                    dve.wait_ge(c_tanh, 1)
                    tick(nc.vector.scalar_tensor_tensor(sil[:].rearrange("p k s -> p s k"),
                                                   c_th[:].rearrange("p (s k) -> p s k", s=2), 1.0,
                                                   vec[:, V_C:V_C + 16].rearrange("p (s k) -> p s k", s=2),
                                                   ALU.add, ALU.mult), sil_ready)
                    settle()
                    nc.vector.tensor_copy(sil0[:, :, 0:2], sil[:])
                    link(nc.vector.tensor_copy(sil4[:, :, 0:2], sil[:]))
                    tick(nc.vector.tensor_tensor(sil4[:, :, 2:4], sil[:], sil4[:, :, 0:2].bitcast(F32),
                                                 ALU.subtract), sil_ready)
                elif s.kind == "mod_turn":
                    full(dve, u[0])
                    bias = vec[:, V_BMOD + 24 * L + s.j0:V_BMOD + 24 * L + s.j0 + s.n]
                    sums_v = tA[:, 0:2 * s.n].rearrange("p (j s) -> p j s", s=2)
                    free(nc.vector.tensor_reduce(sums_v, bank(u[0])[:, 0:4 * s.n].rearrange("p (j a s) -> p j s a", a=2, s=2),
                                                 AX.X, ALU.add), u[0])
                    moved(dve, u[0])
                    link(nc.vector.scalar_tensor_tensor(modv[:, s.j0:s.j0 + s.n, :], sums_v, 0.5,
                                                        bias.unsqueeze(2).to_broadcast([P, s.n, 2]),
                                                        ALU.mult, ALU.add))
                    if s.j0 == 0:
                        g = vec[:, V_NORM + KD * L:V_NORM + KD * (L + 1)]
                        tick(nc.vector.scalar_tensor_tensor(amp[:], modv[:, KD:2 * KD, :], 1.0,
                                                       g.unsqueeze(2).to_broadcast([P, KD, 2]),
                                                       ALU.add, ALU.mult), mod_ready)
                    else:
                        link(nc.vector.tensor_scalar(gatev[:], modv[:, 2 * KD:3 * KD, :], 0.25, None, ALU.mult))
                elif s.kind == "turn_x":
                    if s.k:
                        add_square(0, s.k)
                elif s.kind == "stats":
                    if L:
                        add_square(L, KD - 1)
                    full(dve, u[0])
                    r = s.root
                    ins = nc.vector.tensor_scalar(ms[:, r % 2], bank(u[0])[:, 0:4], 1.0 / D, EPS, ALU.mult, ALU.add)
                    tick(ins, ms_ready)
                    dve.wait_ge(rms_ready, r + 1)
                    free(nc.vector.tensor_copy(tB[:, 0:4], bank(u[0])[:, 0:4]), u[0])
                    for t in range(4):
                        tick(nc.vector.tensor_scalar(diag[:, t], ident[:], rms[:, r % 2, t:t + 1], None, ALU.mult),
                             diag_ready)
                elif s.kind == "spread" and L == 0:
                    dve.wait_ge(rms_spread, 1)
                    for k in range(KD):
                        tick(nc.vector.tensor_tensor(mixed[:, k], xT[:, k], score_ps[:, 0], ALU.mult), scaled)
                elif s.kind == "modulate":
                    if L:
                        dve.wait_ge(rms_spread, 2)
                    for k in range(KD):
                        if L:
                            tick(nc.vector.tensor_tensor(mixed[:, k], xT[:, k], score_ps[:, 0], ALU.mult), scaled)
                        if k > 1:
                            h_lo_part(L, k - 2)
                    for k in (KD - 2, KD - 1):
                        h_lo_part(L, k)
                elif s.kind == "tokens" and s.name != "d_v":
                    nh = 2 if s.name == "b_k" else 4
                    n = nh * HD
                    kd = KINDS.index(s.name)
                    for use, t, q, r in ((u[0], s.t, s.qk, s.root),):
                        dve.wait_ge(sq_ready, r - L)
                        link(nc.vector.tensor_reduce(tA[:, 0:nh], sq[:, 0:n].rearrange("p (h e) -> p h e", e=HD),
                                                     AX.X, ALU.add))
                        tick(nc.vector.tensor_scalar(ms[:, r % 2, 0:nh], tA[:, 0:nh], 1.0 / HD, EPS,
                                                ALU.mult, ALU.add), ms_ready)
                        ps = bank(use)[:, 0:n].rearrange("p (h e) -> p h e", e=HD)
                        tb = tB[:, 0:n].rearrange("p (h e) -> p h e", e=HD)
                        if t < 2:
                            nc.vector.tensor_tensor(tb, ps, rope_g[:, kd, 0, t].unsqueeze(1).to_broadcast([P, nh, HD]),
                                                    ALU.mult)
                            p5 = bank(use)[:, 0:n].rearrange("p (h g s e) -> p h g s e", g=2, s=2, e=16)
                            t5 = tC[:, 0:n].rearrange("p (h g s e) -> p h g s e", g=2, s=2, e=16)
                            sn = rope_g[:, kd, 1, t].rearrange("p (g s e) -> p g s e", g=2, s=2)
                            for h in range(2):
                                ins = nc.vector.tensor_tensor(t5[:, :, :, h], p5[:, :, :, 1 - h],
                                                              sn[:, :, h].unsqueeze(1).to_broadcast([P, nh, 2, 16]),
                                                              ALU.mult)
                            free(ins, use)
                            moved(dve, use)
                            link(nc.vector.tensor_tensor(tB[:, 0:n], tB[:, 0:n], tC[:, 0:n], ALU.add))
                        else:
                            free(nc.vector.tensor_tensor(tb, ps, gains[:, L, kd].unsqueeze(1).to_broadcast([P, nh, HD]),
                                                         ALU.mult), use)
                            moved(dve, use)
                        dve.wait_ge(rms_ready, r + 1)
                        if q >= 4:
                            full(dve, turn_of[q - 4])
                        tick(nc.vector.tensor_tensor(qn[:, q % 4, 0:n].rearrange("p (h e) -> p h e", e=HD), tb,
                                                rms[:, r % 2, 0:nh].unsqueeze(2).to_broadcast([P, nh, HD]),
                                                ALU.mult), qn_ready)
                elif s.kind == "conv":
                    split_lo(s.first_tile + HL + 1)
                    full(dve, u[1])
                    cu = conv_u[:, 0:S]
                    if s.i == 0:
                        nc.vector.memset(conv_u[:, :, 0:1], 0.0)
                        nc.vector.memset(conv_u[:, :, 257:258], 0.0)
                    moved(dve, u[0])
                    free(nc.vector.tensor_tensor(cu[:, :, 1:257], conv_x[:, 0:W].rearrange("p (s t) -> p s t", s=S),
                                                 bank(u[1])[:, 0:W].rearrange("p (s t) -> p s t", s=S), ALU.mult), u[1])
                    moved(dve, u[1])
                    ta = tA[:, 0:W].rearrange("p (s t) -> p s t", s=S)
                    tap = [vec[:, V_CONV + 9 * L + 3 * j + s.i:V_CONV + 9 * L + 3 * j + s.i + 1] for j in range(3)]
                    link(nc.vector.tensor_scalar(ta, cu[:, :, 0:256], tap[0], None, ALU.mult))
                    for j in (1, 2):
                        link(nc.vector.scalar_tensor_tensor(ta, cu[:, :, j:j + 256], tap[j], ta, ALU.mult, ALU.add))
                    split_lo(s.first_tile + HL + 2)
                    full(dve, u[2])
                    free(nc.vector.tensor_tensor(tA[:, 0:W], tA[:, 0:W], bank(u[2])[:, 0:W], ALU.mult), u[2])
                    moved(dve, u[2])
                    split_lo(s.first_tile + HL + 3)
                    z_gate(s, u[3], tA[:, 0:W])
                elif s.kind == "silu":
                    all_moved(dve, u[0])
                    z_gate(s, u[0], y[:, s.i, 0:W])
                elif s.kind == "merge":
                    last_one = s.branch == "a" and s.j == KD - 1
                    for k in range(EARLY) if last_one else ():
                        merged_lo_part(L, k, W)
                    full(dve, u[0])
                    moved(dve, s.gate)
                    gate = gate_t[:, s.n % 2, 0:W]
                    if s.branch == "c":
                        free(nc.vector.scalar_tensor_tensor(mixed[:, s.j, 0:W], gate, 1.0, bank(u[0])[:, 0:W],
                                                            ALU.add, ALU.mult), u[0])
                    else:
                        free(nc.vector.scalar_tensor_tensor(tB[:, 0:W], gate, 1.0, bank(u[0])[:, 0:W],
                                                            ALU.add, ALU.mult), u[0])
                        moved(dve, u[0])
                        ins = nc.vector.tensor_tensor(mixed[:, s.j, 0:W], mixed[:, s.j, 0:W], tB[:, 0:W], ALU.add)
                        tick(ins, mixed_ready if s.branch == "a" else dve_own)
                        if s.branch == "a":
                            for k in range(EARLY, KD) if last_one else ():
                                merged_lo_part(L, k, W)
                elif s.kind == "out":
                    if L == 0 and s.j == 0:
                        rotation_tables(1)
                    full(dve, u[0])
                    for st in range(S):
                        ins = nc.vector.scalar_tensor_tensor(xT[:, s.j, wide(st)], bank(u[0])[:, wide(st)],
                                                             gatev[:, s.j, st:st + 1], xT[:, s.j, wide(st)],
                                                             ALU.mult, ALU.add)
                    free(ins, u[0])
                    if L == 0 and s.j >= 2:
                        settle()
                        add_square(1, s.j - 1)
                elif s.kind == "score":
                    nk = s.kb * P
                    dve.wait_ge(scores_done, s.g + 1)
                    if s.branch == "b" and s.stream == 0:
                        sv = score_ps[:].rearrange("p (e t) k -> p e t k", e=2)
                        for t, c0 in ((0, P), (1, 0)):
                            o = sv[:, :, t, c0:c0 + P]
                            ins = nc.vector.tensor_tensor(o, o, masks[:, t].unsqueeze(1).to_broadcast([P, 2, P]), ALU.add)
                        link(ins)
                    link(nc.vector.tensor_reduce(top, score_ps[:, :, 0:nk], AX.X, ALU.max))
                    if s.branch == "b":
                        c0 = 8 * L + 2 * s.part
                        sink = tail[:, c0:c0 + 2].unsqueeze(2).to_broadcast([P, 2, 2])
                        low_v = low.rearrange("p (e t) -> p e t", e=2)
                        link(nc.vector.scalar_tensor_tensor(low_v, top.rearrange("p (e t) -> p e t", e=2), SCALE, sink,
                                                            ALU.mult, ALU.max))
                        nc.vector.tensor_tensor(sink_d.rearrange("p (e t) -> p e t", e=2), sink, low_v, ALU.subtract)
                        tick(nc.vector.tensor_scalar(negmax, low, -1.0, None, ALU.mult), negmax_ready)
                    else:
                        tick(nc.vector.tensor_scalar(negmax, top, -SCALE, None, ALU.mult), negmax_ready)
                    waiting.append(s)
                elif s.kind == "turn":
                    for i, use in enumerate(u):
                        if i % 2:
                            full(dve, use)
                            e, t = (i // 2, i % 2) if s.branch == "b" else (0, i)
                            free(nc.vector.tensor_copy(
                                probT[:, e, 0:s.kb, t * P:(t + 1) * P],
                                bank(use)[:, 0:s.kb * P].rearrange("p (k q) -> p k q", k=s.kb)), use)
                elif s.kind == "d_root":
                    def clamp(t):
                        tick(nc.vector.tensor_scalar((tB, tC)[t % 2][:], o_d[:, t], BIG, -BIG, ALU.min, ALU.max),
                             o_clamped)

                    all_moved(dve, s.after)
                    clamp(s.toks[0])
                    for i, t in enumerate(s.toks):
                        r = s.root + i
                        dve.wait_ge(sq_ready, r - L)
                        if i + 1 < len(s.toks):
                            clamp(t + 1)
                            settle()
                        link(nc.vector.tensor_reduce(tA[:, 0:4], sq.rearrange("p (h e) -> p h e", e=P),
                                                     AX.X, ALU.add))
                        link(nc.vector.tensor_scalar(tA[:, 4:8], tA[:, 0:4], BIG, BIG / P, ALU.min, ALU.mult))
                        tick(nc.vector.tensor_scalar(ms[:, r % 2], tA[:, 4:8], EPS, None, ALU.add), ms_ready)
                        dve.wait_ge(rms_ready, r + 1)
                        link(nc.vector.scalar_tensor_tensor(tA[:, 8:12], tA[:, 0:4], BIG, rms[:, r % 2],
                                                            ALU.is_lt, ALU.mult))
                        o = o_d[:, t].rearrange("p (h e) -> p h e", e=P)
                        tick(nc.vector.tensor_tensor(o, o, tA[:, 8:12].unsqueeze(2).to_broadcast([P, 4, P]),
                                                     ALU.mult), o_normed)
                if evac_first:
                    split_lo(s.first_tile + HL)


def constants():
    n = np.arange(SEQ)
    seq = 2 * np.pi * ((n[:, None] * n[None, :]) % SEQ) / SEQ
    cs = np.concatenate([np.cos(seq), np.sin(seq)], axis=1).astype(np.float32)
    d = np.arange(HD)
    dim = 2 * np.pi * ((d[:, None] * d[None, :]) % HD) / HD
    norm = 1.0 / math.sqrt(SEQ * HD)
    dft_dim = np.stack([np.kron(np.eye(2), np.cos(dim) * norm), np.kron(np.eye(2), -np.sin(dim) * norm)], axis=1)
    nf = HD // 4
    freq = np.float32(10000.0) ** (-np.arange(nf, dtype=np.float32) / np.float32(nf))
    ar = (n // GRID_W).astype(np.float32)[:, None] * freq[None, :]
    ac = (n % GRID_W).astype(np.float32)[:, None] * freq[None, :]
    cos = np.concatenate([np.cos(ar), np.cos(ar), np.cos(ac), np.cos(ac)], axis=1)
    sin = np.concatenate([-np.sin(ar), np.sin(ar), -np.sin(ac), np.sin(ac)], axis=1)
    rope = np.stack([cos, sin]).reshape(2, 2, P, HD).transpose(2, 0, 1, 3)
    q = np.arange(P)[:, None]
    k = np.arange(P)[None, :]
    masks = np.stack([np.where(k + P - q <= WINDOW, 0.0, MASKED), np.where(q + P - k <= WINDOW, 0.0, MASKED)], axis=1)
    return {
        "ident": np.eye(P, dtype=np.float32),
        "dft_seq": np.ascontiguousarray(cs.reshape(2, P, 2 * SEQ).transpose(1, 0, 2)),
        "dft_dim": np.ascontiguousarray(dft_dim.astype(np.float32)),
        "rope": np.ascontiguousarray(rope.astype(np.float32)),
        "masks": np.ascontiguousarray(masks.astype(np.float32)),
    }


_INS = ["x", "c", "ctx", "c_ctx", "norm_g", "w_mod", "b_mod", "w_in", "q_norm_b", "k_norm_b", "sink_b",
        "conv_w", "q_norm_d", "k_norm_d", "lam_q1", "lam_k1", "lam_q2", "lam_k2", "subln_d",
        "w_o_a", "w_o_b", "w_o_c", "w_o_d", "w_out"]


def kernel(**inputs):
    import concourse.bacc as bacc
    from concourse.bass_utils import run_bass_kernel_spmd

    nc = bacc.Bacc("TRN2", target_bir_lowering=False, num_devices=1)
    arrays, ins, consts = {}, {}, {}
    for name in _INS:
        v = np.ascontiguousarray(inputs[name])
        arrays[f"in_{name}"] = v
        ins[name] = nc.dram_tensor(f"in_{name}", v.shape, mybir.dt.from_np(v.dtype), kind="ExternalInput").ap()
    for name, v in constants().items():
        arrays[f"const_{name}"] = v
        consts[name] = nc.dram_tensor(f"const_{name}", v.shape, mybir.dt.from_np(v.dtype), kind="ExternalInput").ap()
    out = nc.dram_tensor("out_0", (1, SEQ, D), F32, kind="ExternalOutput").ap()
    hybrid_backbone(nc, ins, consts, out)
    r = run_bass_kernel_spmd(nc, [arrays], core_ids=[0])
    return r.results[0]["out_0"]
```
